# Optimizing a Trainium2 kernel written in Bass

```python
import math
import jax
import jax.numpy as jnp
from jax import lax
import numpy as np

D_MODEL = 1024
BATCH = 1
SEQ = 256
DEPTH = 1

N_META = 16
LEAD = 128
N_PAD = LEAD - N_META
M_HEADS = 4
M_HEAD_DIM = D_MODEL // M_HEADS
M_INNER = M_HEADS * M_HEAD_DIM
CONV_W = 4
CHUNK = 64
F_BIAS_LO = 3.0
F_BIAS_HI = 6.0
A_HEADS = 8
A_HEAD_DIM = D_MODEL // (2 * A_HEADS)
A_VDIM = 2 * A_HEAD_DIM
A_INNER = A_HEADS * A_VDIM
Q_BLOCK = 128
N_EXPERTS = 16
N_GROUPS = 4
EXPERTS_PER_GROUP = N_EXPERTS // N_GROUPS
TOP_K = 2
D_EXPERT = D_MODEL
DN_ALPHA = (2 * DEPTH) ** 0.25
DN_BETA = (8 * DEPTH) ** -0.25
LN_EPS = 1e-5
NEG = -1e30
SPLITS = (M_INNER, M_INNER, M_HEADS, M_HEADS, A_INNER, A_INNER, A_INNER, D_MODEL, D_MODEL)
D_IN = 7176

kernel_name = 'hybrid_mlstm_diffattn_groupmoe_block'

def layer_norm(x, g, b):
    xf = x.astype(jnp.float32)
    mu = jnp.mean(xf, axis=-1, keepdims=True)
    var = jnp.mean(jnp.square(xf - mu), axis=-1, keepdims=True)
    y = (xf - mu) * lax.rsqrt(var + LN_EPS) * g.astype(jnp.float32) + b.astype(jnp.float32)
    return y.astype(x.dtype)

def causal_conv(x, w, b):
    y = lax.conv_general_dilated(
        x, w[:, None, :].astype(x.dtype), window_strides=(1,),
        padding=[(CONV_W - 1, 0)], dimension_numbers=('NWC', 'WIO', 'NWC'),
        feature_group_count=x.shape[-1])
    return y + b.astype(x.dtype)

def to_chunks(t):
    bsz, length = t.shape[:2]
    t = t.reshape((bsz, length // CHUNK, CHUNK) + t.shape[2:])
    return jnp.swapaxes(jnp.moveaxis(t, 1, 0), 2, 3)

def mlstm_chunk_step(carry, inp):
    c_state, n_state, m_state = carry
    q, k, v, logi, logf = inp
    causal = jnp.tril(jnp.ones((CHUNK, CHUNK), dtype=bool))
    b = jnp.cumsum(logf, axis=-1)
    g = b[..., -1]
    d_mat = jnp.where(causal, b[..., :, None] - b[..., None, :] + logi[..., None, :], NEG)
    inter = b + m_state[..., None]
    m_t = jnp.maximum(inter, jnp.max(d_mat, axis=-1))
    w_intra = jnp.einsum('bhtd,bhsd->bhts', q, k) * jnp.exp(d_mat - m_t[..., None])
    scale_inter = jnp.exp(inter - m_t)
    num = (jnp.einsum('bhts,bhsv->bhtv', w_intra, v)
           + scale_inter[..., None] * jnp.einsum('bhtd,bhdv->bhtv', q, c_state))
    den = jnp.sum(w_intra, axis=-1) + scale_inter * jnp.einsum('bhtd,bhd->bht', q, n_state)
    h = num / jnp.maximum(jnp.abs(den), jnp.exp(-m_t))[..., None]
    a = g[..., None] - b + logi
    m_new = jnp.maximum(g + m_state, jnp.max(a, axis=-1))
    w_state = jnp.exp(a - m_new[..., None])
    decay = jnp.exp(g + m_state - m_new)
    c_new = decay[..., None, None] * c_state + jnp.einsum('bhs,bhsd,bhsv->bhdv', w_state, k, v)
    n_new = decay[..., None] * n_state + jnp.einsum('bhs,bhsd->bhd', w_state, k)
    return (c_new, n_new, m_new), h

def mlstm_branch(xm, o_pre, i_pre, f_pre, valid, conv_w, conv_b, wq, wk, wv, b_i, b_f, norm_g):
    bsz, length, _ = xm.shape
    f32 = jnp.float32
    xm = xm * valid[None, :, None].astype(xm.dtype)
    xc = jax.nn.silu(causal_conv(xm, conv_w, conv_b))
    xch = xc.reshape(bsz, length, M_HEADS, M_HEAD_DIM)
    xmh = xm.reshape(bsz, length, M_HEADS, M_HEAD_DIM)
    q = jnp.einsum('blhd,hde->blhe', xch, wq).astype(f32)
    k = (jnp.einsum('blhd,hde->blhe', xch, wk) * (M_HEAD_DIM ** -0.5)).astype(f32)
    v = jnp.einsum('blhd,hde->blhe', xmh, wv).astype(f32)
    vmask = valid[None, :, None]
    logi = jnp.where(vmask, i_pre.astype(f32) + b_i.astype(f32), NEG)
    logf = jnp.where(vmask, jax.nn.log_sigmoid(f_pre.astype(f32) + b_f.astype(f32)), 0.0)
    init = (jnp.zeros((bsz, M_HEADS, M_HEAD_DIM, M_HEAD_DIM), f32),
            jnp.zeros((bsz, M_HEADS, M_HEAD_DIM), f32),
            jnp.zeros((bsz, M_HEADS), f32))
    xs = (to_chunks(q), to_chunks(k), to_chunks(v), to_chunks(logi), to_chunks(logf))
    _, h = lax.scan(mlstm_chunk_step, init, xs)
    h = jnp.moveaxis(jnp.swapaxes(h, 2, 3), 0, 1).reshape(bsz, length, M_HEADS, M_HEAD_DIM)
    h = jax.nn.sigmoid(o_pre.astype(f32)).reshape(bsz, length, M_HEADS, M_HEAD_DIM) * h
    mu = jnp.mean(h, axis=-1, keepdims=True)
    var = jnp.mean(jnp.square(h - mu), axis=-1, keepdims=True)
    h = ((h - mu) * lax.rsqrt(var + LN_EPS)).reshape(bsz, length, M_INNER) * norm_g.astype(f32)
    return h.astype(xm.dtype)

def diff_attn_branch(q, k, v, valid, lq1, lk1, lq2, lk2, norm_g, lam_init):
    bsz, length, _ = q.shape
    f32 = jnp.float32
    q = q.reshape(bsz, length, A_HEADS, 2, A_HEAD_DIM) * (A_HEAD_DIM ** -0.5)
    k = k.reshape(bsz, length, A_HEADS, 2, A_HEAD_DIM)
    v = v.reshape(bsz, length, A_HEADS, A_VDIM)
    k1 = k[..., 0, :]
    k2 = k[..., 1, :]
    lam = (jnp.exp(jnp.sum(lq1.astype(f32) * lk1.astype(f32)))
           - jnp.exp(jnp.sum(lq2.astype(f32) * lk2.astype(f32))) + lam_init)
    n_blocks = length // Q_BLOCK
    qb = jnp.moveaxis(q.reshape(bsz, n_blocks, Q_BLOCK, A_HEADS, 2, A_HEAD_DIM), 1, 0)
    starts = jnp.arange(n_blocks) * Q_BLOCK
    kpos = jnp.arange(length)

    def block(args):
        qblk, start = args
        qpos = start + jnp.arange(Q_BLOCK)
        mask = (kpos[None, :] <= qpos[:, None]) & valid[None, :]
        s1 = jnp.einsum('bqhd,bkhd->bhqk', qblk[..., 0, :], k1).astype(f32)
        s2 = jnp.einsum('bqhd,bkhd->bhqk', qblk[..., 1, :], k2).astype(f32)
        a1 = jax.nn.softmax(jnp.where(mask, s1, NEG), axis=-1)
        a2 = jax.nn.softmax(jnp.where(mask, s2, NEG), axis=-1)
        attn = a1 - lam * a2
        return jnp.einsum('bhqk,bkhv->bqhv', attn.astype(v.dtype), v)

    o = lax.map(block, (qb, starts))
    o = jnp.moveaxis(o, 0, 1).reshape(bsz, length, A_HEADS, A_VDIM).astype(f32)
    o = o * lax.rsqrt(jnp.mean(jnp.square(o), axis=-1, keepdims=True) + LN_EPS)
    o = o * norm_g.astype(f32) * (1.0 - lam_init)
    return o.reshape(bsz, length, A_INNER).astype(v.dtype)

def group_moe(x, w_router, router_bias, w_gate, w_up, w_down):
    bsz, length, dm = x.shape
    f32 = jnp.float32
    xt = x.reshape(-1, dm)
    probs = jax.nn.softmax((xt @ w_router).astype(f32), axis=-1)
    sel = probs + router_bias.astype(f32)
    group_score = jnp.max(sel.reshape(-1, N_GROUPS, EXPERTS_PER_GROUP), axis=-1)
    top_group = jnp.argmax(group_score, axis=-1)
    in_group = (jnp.arange(N_EXPERTS) // EXPERTS_PER_GROUP)[None, :] == top_group[:, None]
    _, idx = lax.top_k(jnp.where(in_group, sel, NEG), TOP_K)
    w = jnp.take_along_axis(probs, idx, axis=-1)
    w = w / jnp.sum(w, axis=-1, keepdims=True)
    combine = jnp.einsum('tk,tke->te', w, jax.nn.one_hot(idx, N_EXPERTS, dtype=f32))
    y = jnp.zeros((xt.shape[0], dm), f32)
    for e in range(N_EXPERTS):
        h = jax.nn.silu(xt @ w_gate[e]) * (xt @ w_up[e])
        y = y + combine[:, e:e + 1] * (h @ w_down[e]).astype(f32)
    return y.astype(x.dtype).reshape(bsz, length, dm)

def setup_inputs(seed: int = 0) -> dict:
    key = jax.random.key(seed)
    ks = jax.random.split(key, 32)
    f32 = jnp.float32

    def nrm(k, shape, scale):
        return jax.random.normal(k, shape, f32) * scale

    return {
        'x': nrm(ks[0], (BATCH, SEQ, D_MODEL), 1.0),
        'meta_tokens': nrm(ks[1], (N_META, D_MODEL), 1.0),
        'ln_in_g': 1.0 + nrm(ks[2], (D_MODEL,), 0.02),
        'ln_in_b': nrm(ks[3], (D_MODEL,), 0.02),
        'w_in': nrm(ks[4], (DEPTH, D_MODEL, D_IN), D_MODEL ** -0.5),
        'conv_w': nrm(ks[5], (DEPTH, CONV_W, M_INNER), CONV_W ** -0.5),
        'conv_b': nrm(ks[6], (DEPTH, M_INNER), 0.02),
        'wq_m': nrm(ks[7], (DEPTH, M_HEADS, M_HEAD_DIM, M_HEAD_DIM), M_HEAD_DIM ** -0.5),
        'wk_m': nrm(ks[8], (DEPTH, M_HEADS, M_HEAD_DIM, M_HEAD_DIM), M_HEAD_DIM ** -0.5),
        'wv_m': nrm(ks[9], (DEPTH, M_HEADS, M_HEAD_DIM, M_HEAD_DIM), M_HEAD_DIM ** -0.5),
        'b_i': nrm(ks[10], (DEPTH, M_HEADS), 0.1),
        'b_f': jnp.linspace(F_BIAS_LO, F_BIAS_HI, M_HEADS, dtype=f32)[None, :] + nrm(ks[11], (DEPTH, M_HEADS), 0.1),
        'm_norm_g': 1.0 + nrm(ks[12], (DEPTH, M_INNER), 0.02),
        'lam_q1': nrm(ks[13], (DEPTH, A_HEAD_DIM), 0.1),
        'lam_k1': nrm(ks[14], (DEPTH, A_HEAD_DIM), 0.1),
        'lam_q2': nrm(ks[15], (DEPTH, A_HEAD_DIM), 0.1),
        'lam_k2': nrm(ks[16], (DEPTH, A_HEAD_DIM), 0.1),
        'a_norm_g': 1.0 + nrm(ks[17], (DEPTH, A_VDIM), 0.02),
        'w_branch_m': nrm(ks[18], (DEPTH, M_INNER, D_MODEL), M_INNER ** -0.5),
        'w_branch_a': nrm(ks[19], (DEPTH, A_INNER, D_MODEL), A_INNER ** -0.5),
        'w_out': nrm(ks[20], (DEPTH, D_MODEL, D_MODEL), D_MODEL ** -0.5 * DN_BETA),
        'ln1_g': 1.0 + nrm(ks[21], (DEPTH, D_MODEL), 0.02),
        'ln1_b': nrm(ks[22], (DEPTH, D_MODEL), 0.02),
        'ln2_g': 1.0 + nrm(ks[23], (DEPTH, D_MODEL), 0.02),
        'ln2_b': nrm(ks[24], (DEPTH, D_MODEL), 0.02),
        'w_router': nrm(ks[25], (D_MODEL, N_EXPERTS), D_MODEL ** -0.5),
        'router_bias': nrm(ks[26], (N_EXPERTS,), 0.01),
        'w_gate_e': nrm(ks[27], (DEPTH, N_EXPERTS, D_MODEL, D_EXPERT), D_MODEL ** -0.5),
        'w_up_e': nrm(ks[28], (DEPTH, N_EXPERTS, D_MODEL, D_EXPERT), D_MODEL ** -0.5),
        'w_down_e': nrm(ks[29], (DEPTH, N_EXPERTS, D_EXPERT, D_MODEL), D_EXPERT ** -0.5 * DN_BETA),
    }

def reference(x, meta_tokens, ln_in_g, ln_in_b, w_in, conv_w, conv_b, wq_m, wk_m, wv_m,
              b_i, b_f, m_norm_g, lam_q1, lam_k1, lam_q2, lam_k2, a_norm_g,
              w_branch_m, w_branch_a, w_out, ln1_g, ln1_b, ln2_g, ln2_b,
              w_router, router_bias, w_gate_e, w_up_e, w_down_e):
    bsz, seq, dm = x.shape
    length = seq + LEAD
    pad = jnp.zeros((bsz, N_PAD, dm), x.dtype)
    meta = jnp.broadcast_to(meta_tokens[None].astype(x.dtype), (bsz, N_META, dm))
    h = jnp.concatenate([pad, meta, x], axis=1)
    valid = jnp.arange(length) >= N_PAD
    h = layer_norm(h, ln_in_g, ln_in_b)
    split_points = [int(s) for s in np.cumsum(SPLITS)[:-1]]
    for l in range(DEPTH):
        proj = h @ w_in[l]
        xm, o_pre, i_pre, f_pre, qa, ka, va, ga, gb = jnp.split(proj, split_points, axis=-1)
        y_m = mlstm_branch(xm, o_pre, i_pre, f_pre, valid, conv_w[l], conv_b[l],
                           wq_m[l], wk_m[l], wv_m[l], b_i[l], b_f[l], m_norm_g[l])
        lam_init = 0.8 - 0.6 * math.exp(-0.3 * l)
        y_a = diff_attn_branch(qa, ka, va, valid, lam_q1[l], lam_k1[l], lam_q2[l], lam_k2[l],
                               a_norm_g[l], lam_init)
        merged = jax.nn.sigmoid(ga) * (y_m @ w_branch_m[l]) + jax.nn.sigmoid(gb) * (y_a @ w_branch_a[l])
        h = layer_norm(DN_ALPHA * h + merged @ w_out[l], ln1_g[l], ln1_b[l])
        ffn = group_moe(h, w_router, router_bias, w_gate_e[l], w_up_e[l], w_down_e[l])
        h = layer_norm(DN_ALPHA * h + ffn, ln2_g[l], ln2_b[l])
    return h[:, LEAD:]


_drawn_inputs = setup_inputs


def setup_inputs(seed=0):
    import zlib

    import numpy as np

    out = dict(_drawn_inputs(seed))
    spreads = {}
    factors = {'conv_b': 5.668, 'b_i': 64.0, 'a_norm_g': 2.858, 'ln2_g': 8.446, 'ln2_b': 8.276}
    for name, (base, spread) in spreads.items():
        noise = np.random.default_rng([zlib.crc32(name.encode()), seed]).standard_normal(out[name].shape)
        drawn = base * np.exp(spread * noise) if base else spread * noise
        out[name] = jnp.asarray(drawn.astype(out[name].dtype))
    for name, factor in factors.items():
        out[name] = (out[name] * factor).astype(out[name].dtype)
    return out
```

```python
import math
from contextlib import ExitStack


import concourse.bass as bass
from concourse import mybir

F32 = mybir.dt.float32
F32R = mybir.dt.float32r
I32 = mybir.dt.int32
ALU = mybir.AluOpType
ACT = mybir.ActivationFunctionType
AX = mybir.AxisListType

P = 128
D = 1024
KB = D // P
META = 16
T = 256
S = META + T
TT = T // P
STILES = ((0, P), (P, P), (2 * P, META))
MH, MD = 4, 256
AH, AD, AV = 8, 64, 128
CONV = 4
NE, NG, EPG = 16, 4, 4
SLOTS = 64
MAXBLK = T // SLOTS
D_IN = 7176
ALPHA = 2.0 ** 0.25
LAM_INIT = 0.8 - 0.6 * math.exp(-0.3 * 0)
EPS = 1e-5
BIG = 1e30

XM, OG, KA, QA, VA, GA, WM, GB, WA = range(9)
COLUMN = {XM: 0, OG: 1024, QA: 2056, KA: 3080, VA: 4104, GA: 5128, GB: 6152}
MATRICES = [XM, OG, "heads", KA, QA, VA, GA, WM, GB, WA, "out"]
PIECES = 2 * KB
NBUF = 4
OUT_BASE = PIECES * 9
FIRST_E = len(MATRICES)
LAP = [(FIRST_E + j) // 3 - ((FIRST_E + j) % 3 == MATRICES.index("heads") % 3) for j in range(3)]
ESLOT = [(FIRST_E + j) % 3 for j in range(3)]


def slot_of(section):
    return MATRICES.index(section) % 3


def lap_of(section):
    m, heads = MATRICES.index(section), MATRICES.index("heads")
    return m // 3 + 1 - (m > heads and m % 3 == heads % 3)


class Semaphores:
    pass


class Steps:

    def __init__(self, eng, sem):
        self.eng, self.sem, self.n, self.base = eng, sem, 0, 0

    def __call__(self, ins):
        self.n += 1
        return ins.then_inc(self.sem, 1)

    def settle(self):
        self.eng.wait_ge(self.sem, self.base + self.n)


def build(ctx, nc, x, meta, ln_in_g, ln_in_b, w_in, conv_w, conv_b, wq, wk, wv, b_i, b_f, m_norm_g,
          lam_q1, lam_k1, lam_q2, lam_k2, a_norm_g, w_bm, w_ba, w_out, ln1_g, ln1_b, ln2_g, ln2_b,
          w_router, router_bias, w_gate, w_up, w_down, out):
    top = [(nc.sbuf_base + 63) // 64 * 64]

    def bytes_of(shape):
        n = 4
        for d in shape[1:]:
            n *= d
        return n

    def perm(name, shape, dt=F32):
        t = nc.alloc_sbuf_tensor_at(name, shape, dt, offset=top[0])
        top[0] += (bytes_of(shape) + 31) // 32 * 32
        return t

    raw = perm("raw", [P, 3, KB, D])
    whi = perm("whi", [P, NBUF, 4 * P], F32R)
    wlo = perm("wlo", [P, NBUF, 4 * P], F32R)
    ident = perm("ident", [P, P])
    late = perm("late", [P, P])
    ahead = perm("ahead", [P, P])
    before = perm("before", [P, P])
    ones = perm("ones", [P, P])
    slotno = perm("slotno", [P, 2, SLOTS])
    sel = perm("sel", [MH, MH, P])
    boff = perm("boff", [P, MAXBLK])
    minus_half = perm("minus_half", [P, 2 * AH])
    rank16 = perm("rank16", [P, NE])
    chan = perm("chan", [P, 65])
    mrow = perm("mrow", [MH, S])
    at_col = perm("at_col", [P, 3, MH])
    em_col = perm("em_col", [P, TT, MH])
    gate_bias = perm("gate_bias", [MH, 2])
    wr = perm("wr", [P, KB, NE])
    rbias = perm("rbias", [P, NE])
    stats = perm("stats", [P, 3, 2, 6])
    mv = perm("mv", [P, 3, 2])
    ve = perm("ve", [P, 3])
    rstd = perm("rstd", [P, 3])
    stats8 = perm("stats8", [P, TT * MH, 6])
    mv8 = perm("mv8", [P, TT * MH, 2])
    ve8 = perm("ve8", [P, TT * MH])
    rstd8 = perm("rstd8", [P, TT * MH])
    den = perm("den", [P, MH, TT])
    rden = perm("rden", [P, MH, TT])
    neglam = perm("neglam", [P, 1])
    nmax = perm("nmax", [P, 2, TT, 2])
    rsum = perm("rsum", [P, 2, TT, 2])
    rinv = perm("rinv", [P, 2, TT, 2])
    ssq = perm("ssq", [P, TT * AH])
    vea = perm("vea", [P, TT * AH])
    rstda = perm("rstda", [P, TT * AH])
    work = (top[0] + 63) // 64 * 64

    def at(name, shape, offset, dt=F32):
        return nc.alloc_sbuf_tensor_at(name, shape, dt, offset=work + offset)

    hi_h = at("hi_h", [P, KB, S], 0, F32R)
    lo_h = at("lo_h", [P, KB, S], 8704, F32R)
    hres = at("hres", [P, TT, D], 17408)
    F = 25600
    xt = at("xt", [P, 3, D], F)
    rows_in = at("rows_in", [P, 2, D], F + 12288)
    hfull = at("hfull", [P, 2, S], F + 20480)
    crow = at("crow", [65, P], F + 22656)
    lamv = at("lamv", [P, 4, AD], F + 23168)
    lamp = at("lamp", [P, 2, AD], F + 24192)
    lams = at("lams", [P, 4], F + 24704)
    wif = at("wif", [P, KB, 2 * MH], F + 24736)
    wif_hi = at("wif_hi", [P, KB, 64], F + 24992, F32R)
    wif_lo = at("wif_lo", [P, KB, 64], F + 27040, F32R)
    qm = at("qm", [P, KB, T], F)
    km = at("km", [P, KB, S], F + 8192)
    vm = at("vm", [P, 3, MH, MD + 1], F + 16896)
    xm = at("xm", [P, KB, S + CONV - 1], F + 29248)
    xc = at("xc", [P, KB, S], F + 38048)
    ot = at("ot", [P, KB, T], F + 46752)
    SCAN = 2 * P
    scan = at("scan", [MH, 3, SCAN + S], F + 55296)
    gtmp = at("gtmp", [MH, 2, S], F + 61632)
    wgt = at("wgt", [P, 2, 3, T], F + 29248)
    ex = at("ex", [P, 2, 416], F + 35392)
    csig = at("csig", [P, 2, S], F + 16896)
    hh = at("hh", [P, TT, D], F + 55296)
    ka = at("ka", [P, KB, S], F)
    qa = at("qa", [P, 2, KB, T], F + 8704)
    vat = at("vat", [P, KB, S], F + 25088)
    oall = at("oall", [P, TT, D], F + 25088)
    va = at("va", [P, 3, D], F + 33792)
    ea = at("ea", [P, 2, 2, 416], F + 46080)
    att = at("att", [P, 3 * P], F + 52736)
    att2 = at("att2", [META, 2 * P], F + 54272)
    junk = (at("junk0", [P, P], F + 33280), at("junk1", [P, P], F + 63488))
    ym_hi = at("ym_hi", [P, KB, T], F, F32R)
    ym_lo = at("ym_lo", [P, KB, T], F + 8192, F32R)
    ya_hi = at("ya_hi", [P, KB, T], F + 33792, F32R)
    ya_lo = at("ya_lo", [P, KB, T], F + 41984, F32R)
    sg = at("sg", [P, KB, T], F + 16384)
    merged = at("merged", [P, KB, T], F + 24576)
    mtmp = at("mtmp", [P, 2, T], F + 50176)
    mg_hi = at("mg_hi", [P, KB, T], 0, F32R)
    mg_lo = at("mg_lo", [P, KB, T], 8192, F32R)
    h1 = at("h1", [P, TT, D], F)
    acc = at("acc", [P, TT, D], F + 8192)
    h1t = at("h1t", [P, KB, T], F + 24576)
    lgt = at("lgt", [NE, T], F + 16384)
    rt = at("rt", [P, 16, TT * NE], F + 17408)
    gsb = at("gsb", [P, D], F + 32768)
    usb = at("usb", [P, D], F + 36864)
    gate = at("gate", [P, KB, SLOTS], F + 40960)
    gsig = at("gsig", [P, KB, SLOTS], F + 43008)
    upv = at("upv", [P, KB, SLOTS], F + 45056)
    hid = at("hid", [P, KB, SLOTS], F + 47104)
    mask = at("mask", [P, TT, NE], F + 52224)
    comb = at("comb", [P, TT, NE], F + 52352)
    slot = at("slot", [P, TT, NE], F + 52480)
    counts = at("counts", [1, NE], F + 52608)
    nblk_f = at("nblk_f", [1, NE], F + 52672)
    ends_f = at("ends_f", [1, 2, 32 + NE], F + 52736)
    units = at("units", [1, 3, NE], F + 53120, I32)
    zsb = at("zsb", [P, D], 17408)
    xg = at("xg", [P, KB, SLOTS], 17408 + 4096)
    pick = at("pick", [P, TT, 2 * SLOTS], 17408 + 6144)
    wpick = at("wpick", [P, TT, 2 * SLOTS], 17408 + 7168)
    wpt = at("wpt", [P, TT, P], 0)
    rows1 = at("rows1", [P, 2, D], F + 55296)

    ps = nc.alloc_psum_tensor("ps", [P, 8, 512], F32)

    s = Semaphores()
    s.x_in0 = nc.alloc_semaphore("x_in0")
    s.x_in1 = nc.alloc_semaphore("x_in1")
    s.x_in2 = nc.alloc_semaphore("x_in2")
    s.crow_in = nc.alloc_semaphore("crow_in")
    s.rows_in_in = nc.alloc_semaphore("rows_in_in")
    s.gb_in = nc.alloc_semaphore("gb_in")
    s.lam_in = nc.alloc_semaphore("lam_in")
    s.wif_in = nc.alloc_semaphore("wif_in")
    s.wr_in = nc.alloc_semaphore("wr_in")
    s.rb_in = nc.alloc_semaphore("rb_in")
    s.heads_in = nc.alloc_semaphore("heads_in")
    s.rows1_in = nc.alloc_semaphore("rows1_in")
    s.rows2_in = nc.alloc_semaphore("rows2_in")
    s.stored = nc.alloc_semaphore("stored")
    s.consts = nc.alloc_semaphore("consts")
    s.dve = nc.alloc_semaphore("dve")
    s.act = nc.alloc_semaphore("act")
    s.pool = nc.alloc_semaphore("pool")
    s.xn_ready = nc.alloc_semaphore("xn_ready")
    s.var_ready = nc.alloc_semaphore("var_ready")
    s.rstd_ready = nc.alloc_semaphore("rstd_ready")
    s.hres_ready = nc.alloc_semaphore("hres_ready")
    s.rows_t = nc.alloc_semaphore("rows_t")
    s.chan_ready = nc.alloc_semaphore("chan_ready")
    s.ht_t = nc.alloc_semaphore("ht_t")
    s.h_full = nc.alloc_semaphore("h_full")
    s.h_hi = nc.alloc_semaphore("h_hi")
    s.h_lo = nc.alloc_semaphore("h_lo")
    s.wif_split = nc.alloc_semaphore("wif_split")
    s.if_done = nc.alloc_semaphore("if_done")
    s.hi_ready = nc.alloc_semaphore("hi_ready")
    s.lo_ready = nc.alloc_semaphore("lo_ready")
    s.pieces_used = nc.alloc_semaphore("pieces_used")
    s.conv_acc = nc.alloc_semaphore("conv_acc")
    s.conv_sig = nc.alloc_semaphore("conv_sig")
    s.xc_ready = nc.alloc_semaphore("xc_ready")
    s.hp_done = nc.alloc_semaphore("hp_done")
    s.hp_act = nc.alloc_semaphore("hp_act")
    s.ot_t = nc.alloc_semaphore("ot_t")
    s.ot_ready = nc.alloc_semaphore("ot_ready")
    s.gates_ready = nc.alloc_semaphore("gates_ready")
    s.gates_t = nc.alloc_semaphore("gates_t")
    s.aux_ready = nc.alloc_semaphore("aux_ready")
    s.scan_e = nc.alloc_semaphore("scan_e")
    s.scan_l = nc.alloc_semaphore("scan_l")
    s.exp_ready = nc.alloc_semaphore("exp_ready")
    s.mb_done = nc.alloc_semaphore("mb_done")
    s.sc_done = nc.alloc_semaphore("sc_done")
    s.e_done = nc.alloc_semaphore("e_done")
    s.w_done = nc.alloc_semaphore("w_done")
    s.num_done = nc.alloc_semaphore("num_done")
    s.hh_done = nc.alloc_semaphore("hh_done")
    s.var8 = nc.alloc_semaphore("var8")
    s.rstd8_ready = nc.alloc_semaphore("rstd8_ready")
    s.hn_ready = nc.alloc_semaphore("hn_ready")
    s.vm_ones = nc.alloc_semaphore("vm_ones")
    s.qa_zero = nc.alloc_semaphore("qa_zero")
    s.va_t = nc.alloc_semaphore("va_t")
    s.va_ready = nc.alloc_semaphore("va_ready")
    s.lam_sum = nc.alloc_semaphore("lam_sum")
    s.lam_exp = nc.alloc_semaphore("lam_exp")
    s.s_done = nc.alloc_semaphore("s_done")
    s.nmax_done = nc.alloc_semaphore("nmax_done")
    s.exp_done = nc.alloc_semaphore("exp_done")
    s.attn_done = nc.alloc_semaphore("attn_done")
    s.tr_done = nc.alloc_semaphore("tr_done")
    s.at_act = nc.alloc_semaphore("at_act")
    s.at_dve = nc.alloc_semaphore("at_dve")
    s.av_done = nc.alloc_semaphore("av_done")
    s.o_copied = nc.alloc_semaphore("o_copied")
    s.o_squared = nc.alloc_semaphore("o_squared")
    s.vara = nc.alloc_semaphore("vara")
    s.rstda_ready = nc.alloc_semaphore("rstda_ready")
    s.ya_ready = nc.alloc_semaphore("ya_ready")
    s.ym_t = nc.alloc_semaphore("ym_t")
    s.ym_hi_s = nc.alloc_semaphore("ym_hi_s")
    s.ym_lo_s = nc.alloc_semaphore("ym_lo_s")
    s.ya_t = nc.alloc_semaphore("ya_t")
    s.ya_hi_s = nc.alloc_semaphore("ya_hi_s")
    s.ya_lo_s = nc.alloc_semaphore("ya_lo_s")
    s.ym_full = nc.alloc_semaphore("ym_full")
    s.ya_full = nc.alloc_semaphore("ya_full")
    s.merged_s = nc.alloc_semaphore("merged_s")
    s.mg_hi_s = nc.alloc_semaphore("mg_hi_s")
    s.mg_lo_s = nc.alloc_semaphore("mg_lo_s")
    s.resid_done = nc.alloc_semaphore("resid_done")
    s.var1 = nc.alloc_semaphore("var1")
    s.rstd1 = nc.alloc_semaphore("rstd1")
    s.h1_ready = nc.alloc_semaphore("h1_ready")
    s.acc_ready = nc.alloc_semaphore("acc_ready")
    s.h1_t = nc.alloc_semaphore("h1_t")
    s.h1t_act = nc.alloc_semaphore("h1t_act")
    s.h1t_dve = nc.alloc_semaphore("h1t_dve")
    s.logit_done = nc.alloc_semaphore("logit_done")
    s.logit_sb = nc.alloc_semaphore("logit_sb")
    s.logit_t = nc.alloc_semaphore("logit_t")
    s.router_exp = nc.alloc_semaphore("router_exp")
    s.exp_r = nc.alloc_semaphore("exp_r")
    s.mask_ready = nc.alloc_semaphore("mask_ready")
    s.rank_done = nc.alloc_semaphore("rank_done")
    s.units_ready = nc.alloc_semaphore("units_ready")
    s.pick_ready = nc.alloc_semaphore("pick_ready")
    s.gath_done = nc.alloc_semaphore("gath_done")
    s.xg_ready = nc.alloc_semaphore("xg_ready")
    s.gate_used = nc.alloc_semaphore("gate_used")
    s.up_used = nc.alloc_semaphore("up_used")
    s.down_used = nc.alloc_semaphore("down_used")
    s.gsb_ready = nc.alloc_semaphore("gsb_ready")
    s.tg_done = nc.alloc_semaphore("tg_done")
    s.gate_ready = nc.alloc_semaphore("gate_ready")
    s.gsig_ready = nc.alloc_semaphore("gsig_ready")
    s.usb_ready = nc.alloc_semaphore("usb_ready")
    s.tu_done = nc.alloc_semaphore("tu_done")
    s.hid_ready = nc.alloc_semaphore("hid_ready")
    s.scat_done = nc.alloc_semaphore("scat_done")
    s.acc_added = nc.alloc_semaphore("acc_added")
    s.wpt_t = nc.alloc_semaphore("wpt_t")
    s.wpt_ready = nc.alloc_semaphore("wpt_ready")
    s.z_ready = nc.alloc_semaphore("z_ready")
    s.wpick_ready = nc.alloc_semaphore("wpick_ready")
    s.moe_dve = nc.alloc_semaphore("moe_dve")
    s.fin_var = nc.alloc_semaphore("fin_var")
    s.fin_rstd = nc.alloc_semaphore("fin_rstd")
    s.fin_ready = nc.alloc_semaphore("fin_ready")
    raw_in = [[nc.alloc_semaphore(f"raw_in_{a}_{q}") for q in range(4)] for a in range(3)]
    evac = [nc.alloc_semaphore(f"evac_{n}") for n in range(9)]

    block = ctx.enter_context(nc.Block())

    def raw_quarter(slot_no, q):
        return raw[:, slot_no, 2 * q:2 * q + 2, :]

    def rows_of(w, q):
        return w[256 * q:256 * q + 256, :].rearrange("(j p) c -> p j c", p=P)

    def piece(section, blk, kh):
        a = slot_of(section)
        return raw[:, a, 4 * kh:4 * kh + 4, bass.ds(blk * P, P)]

    def out_piece(n):
        return raw[:, slot_of("out"), n // 2, 512 * (n % 2):512 * (n % 2) + 512]

    def bank(section, blk_odd):
        return 2 * (section % 2) + blk_odd

    def c_conv(w, blk):
        return chan[:, bass.ds(w * KB + blk, 1)]

    C_CONVB, C_LNG, C_LNB, C_MG, C_AG = 32, 40, 48, 56, 64

    @block.sync
    def _(sp):
        dram = {WM: w_bm[0], WA: w_ba[0], "out": w_out[0]}
        free = {KA: ("lo", 1), QA: ("lo", 2), VA: ("heads", 0), GA: ("lo", 3), WM: ("lo", 4),
                GB: ("lo", 5), WA: ("lo", 6), "out": ("lo", 7)}
        for m, what in enumerate(MATRICES):
            if what == "heads":
                for j, w in enumerate((wq, wk, wv)):
                    sp.dma_start(raw[:, m % 3, 2 * j:2 * j + 2, :].rearrange("p a (b e) -> p (a b) e", e=MD),
                                 w[0].rearrange("h (c p) e -> p (h c) e", p=P)).then_inc(s.heads_in, 16)
                continue
            if what in free:
                kind, done = free[what]
                if kind == "lo":
                    sp.wait_ge(s.lo_ready, PIECES * done)
                else:
                    sp.wait_ge(s.hp_done, 28)
            for q in range(4):
                if what in dram:
                    src = rows_of(dram[what], q)
                else:
                    src = rows_of(w_in[0, :, COLUMN[what]:COLUMN[what] + D], q)
                sp.dma_start(raw_quarter(m % 3, q), src).then_inc(raw_in[m % 3][q], 16)

        for j, (w, done) in enumerate(((w_gate, 8), (w_up, 9), (w_down, 10))):
            sp.wait_ge(s.lo_ready, PIECES * done)
            for q in range(4):
                sp.dma_start(raw_quarter(ESLOT[j], q), rows_of(w[0, 0], q)).then_inc(raw_in[ESLOT[j]][q], 16)
        sp.wait_ge(s.units_ready, 1)
        with sp.Fori(1, NE) as e:
            last = sp.value_load(units[0:1, 2, bass.ds(e - 1, 1)], min_val=0, max_val=NE * MAXBLK)
            for j, (w, used) in enumerate(((w_gate, s.gate_used), (w_up, s.up_used), (w_down, s.down_used))):
                for q in range(4):
                    sp.wait_ge(used, last * 4 + (q + 1))
                    src = w[0, bass.ds(e, 1), 256 * q:256 * q + 256, :].rearrange("e (j p) c -> p (e j) c", p=P)
                    sp.dma_start(raw_quarter(ESLOT[j], q), src).then_inc(raw_in[ESLOT[j]][q], 16)
        for t in range(TT):
            sp.wait_ge(s.fin_ready, t + 1)
            sp.dma_start(out[0, P * t:P * t + P, :], acc[:, t, :]).then_inc(s.stored, 16)
        sp.wait_ge(s.stored, 16 * TT)

    @block.gpsimd
    def _(pool):
        own = Steps(pool, s.pool)
        for t, v in ((ident, 0.0), (late, 0.0), (ahead, 0.0), (before, 1.0), (sel, 0.0), (ones, 1.0),
                     (minus_half, -0.5)):
            own(pool.memset(t[:], v))
        own(pool.memset(wif_hi[:].bitcast(F32), 0.0))
        own(pool.memset(wif_lo[:].bitcast(F32), 0.0))
        own(pool.memset(xm[:, :, 0:CONV - 1], 0.0))
        own(pool.iota(slotno[:], pattern=[[0, 2], [1, SLOTS]], base=0, channel_multiplier=0,
                      allow_small_or_imprecise_dtypes=True))
        own(pool.iota(boff[:], pattern=[[SLOTS, MAXBLK]], base=0, channel_multiplier=0,
                      allow_small_or_imprecise_dtypes=True))
        own(pool.iota(rank16[:], pattern=[[-1, NE]], base=NE, channel_multiplier=0,
                      allow_small_or_imprecise_dtypes=True))
        own.settle()
        own(pool.affine_select(out=ident[:], in_=ident[:], compare_op=ALU.not_equal, fill=1.0, base=0,
                               pattern=[[-1, P]], channel_multiplier=1))
        own(pool.affine_select(out=late[:], in_=late[:], compare_op=ALU.is_gt, fill=BIG, base=1,
                               pattern=[[1, P]], channel_multiplier=-1))
        own(pool.affine_select(out=ahead[:], in_=ahead[:], compare_op=ALU.is_gt, fill=-BIG, base=1,
                               pattern=[[-1, P]], channel_multiplier=1))
        own(pool.affine_select(out=before[:], in_=before[:], compare_op=ALU.is_gt, fill=0.0, base=0,
                               pattern=[[1, P]], channel_multiplier=-1))
        own(pool.affine_select(out=sel[:], in_=sel[:], compare_op=ALU.not_equal, fill=1.0, base=0,
                               pattern=[[-1, MH], [0, P]], channel_multiplier=1))
        own.settle()
        pool.drain().then_inc(s.consts, 1)
        pool.wait_ge(s.var_ready, 3)
        pool.tensor_tensor(rstd[0:META, 0:1], ve[0:META, 0:1], minus_half[0:META, 0:1],
                           ALU.pow).then_inc(s.rstd_ready, 1)
        pool.tensor_tensor(rstd[:, 1:3], ve[:, 1:3], minus_half[:, 1:3], ALU.pow).then_inc(s.rstd_ready, 1)
        pool.wait_ge(s.xn_ready, 3)
        pool.wait_ge(s.rows_in_in, 32)
        own(pool.tensor_tensor(hres[:], xt[:, 1:3, :], rows_in[:, 0, :].unsqueeze(1).to_broadcast([P, TT, D]),
                               ALU.mult))
        own.settle()
        pool.tensor_tensor(hres[:], hres[:], rows_in[:, 1, :].unsqueeze(1).to_broadcast([P, TT, D]),
                           ALU.add).then_inc(s.hres_ready, 1)
        pool.sem_inc(s.xc_ready, 2)
        with pool.Fori(0, KB // 2) as i:
            for j in range(2):
                pool.wait_ge(s.conv_sig, i * 2 + (j + 1))
                pool.tensor_tensor(xc[:, bass.ds(i * 2 + j, 1), :], xc[:, bass.ds(i * 2 + j, 1), :],
                                   csig[:, j:j + 1, :], ALU.mult).then_inc(s.xc_ready, 1)
        pool.wait_ge(s.if_done, 1)
        pool.wait_ge(s.xc_ready, KB + 2)
        pool.memset(vm[:, :, :, MD:MD + 1], 1.0).then_inc(s.vm_ones, 1)
        pool.wait_ge(s.hp_done, 28)
        for b in range(2):
            pool.memset(wgt[:, b, 1, 0:112], 0.0).then_inc(s.vm_ones, 1)
            pool.wait_ge(s.vm_ones, 2 + 2 * b)
            pool.memset(wgt[0:META, b, 2, 0:240], 0.0).then_inc(s.vm_ones, 1)
            pool.wait_ge(s.vm_ones, 3 + 2 * b)
        pool.wait_ge(s.var8, 1)
        pool.tensor_tensor(rstd8[:], ve8[:], minus_half[:, 0:TT * MH], ALU.pow).then_inc(s.rstd8_ready, 1)
        pool.wait_ge(s.num_done, MH)
        pool.wait_ge(s.rstd8_ready, 1)
        pool.memset(qa[AD:P, 0, :, :], 0.0).then_inc(s.qa_zero, 1)
        pool.wait_ge(s.qa_zero, 1)
        pool.memset(qa[0:AD, 1, :, :], 0.0).then_inc(s.qa_zero, 1)
        pool.wait_ge(s.qa_zero, 2)
        pool.wait_ge(s.vara, 1)
        pool.tensor_tensor(rstda[:], vea[:], minus_half[:], ALU.pow).then_inc(s.rstda_ready, 1)
        pool.wait_ge(s.var1, 1)
        pool.tensor_tensor(rstd[:, 0:2], ve[:, 0:2], minus_half[:, 0:2], ALU.pow).then_inc(s.rstd1, 1)
        pool.wait_ge(s.resid_done, 1)
        pool.memset(zsb[:], 0.0).then_inc(s.z_ready, 2)
        pool.memset(wpt[:], 0.0).then_inc(s.wpt_ready, 1)
        pool.wait_ge(s.fin_var, 1)
        pool.tensor_tensor(rstd[:, 0:2], ve[:, 0:2], minus_half[:, 0:2], ALU.pow).then_inc(s.fin_rstd, 1)

    @block.scalar
    def _(act):
        for j in range(3):
            src = meta if j == 0 else x[0, P * (j - 1):P * j, :]
            act.dma_start(xt[0:src.shape[0], j, :], src).then_inc((s.x_in0, s.x_in1, s.x_in2)[j], 16)
        for r0, v in ((0, conv_w[0].rearrange("w (b c) -> (w b) c", c=P)), (32, conv_b[0].rearrange("(b c) -> b c", c=P)),
                      (40, ln_in_g.rearrange("(b c) -> b c", c=P)), (48, ln_in_b.rearrange("(b c) -> b c", c=P)),
                      (56, m_norm_g[0].rearrange("(b c) -> b c", c=P)), (64, a_norm_g)):
            act.dma_start(crow[r0:r0 + v.shape[0], :], v).then_inc(s.crow_in, 16)
        for j, v in enumerate((ln_in_g, ln_in_b)):
            act.dma_start(rows_in[:, j, :], v.partition_broadcast(P)).then_inc(s.rows_in_in, 16)
        with nc.allow_non_contiguous_dma(reason="a few short vectors"):
            act.dma_start(wif[:], w_in[0, :, 2048:2056].rearrange("(k p) c -> p k c", p=P)).then_inc(s.wif_in, 16)
            act.dma_start(gate_bias[:, 0:1], b_i.rearrange("a h -> h a")).then_inc(s.gb_in, 16)
            act.dma_start(gate_bias[:, 1:2], b_f.rearrange("a h -> h a")).then_inc(s.gb_in, 16)
        for j, v in enumerate((lam_q1, lam_q2, lam_k1, lam_k2)):
            act.dma_start(lamv[:, j, :], v[0].partition_broadcast(P)).then_inc(s.lam_in, 16)
        act.dma_start(wr[:], w_router.rearrange("(k p) e -> p k e", p=P)).then_inc(s.wr_in, 16)
        act.dma_start(rbias[:], router_bias.partition_broadcast(P)).then_inc(s.rb_in, 16)

        act.wait_ge(s.lam_sum, 1)
        act.activation(lams[:, 2:4], lams[:, 0:2], ACT.Exp).then_inc(s.lam_exp, 1)
        for k in range(KB):
            act.wait_ge(s.h_full, k + 1)
            act.copy(hi_h[:, k, :], hfull[:, k % 2, :]).then_inc(s.h_hi, 1)
        act.wait_ge(s.wif_in, 16)
        act.wait_ge(s.consts, 1)
        act.copy(wif_hi[:, :, 0:MH], wif[:, :, MH:2 * MH]).then_inc(s.wif_split, 1)
        act.copy(wif_hi[:, :, 32:32 + MH], wif[:, :, 0:MH]).then_inc(s.wif_split, 1)

        def split(section, blk, odd):
            if isinstance(blk, int) and blk == 0:
                for q in range(4):
                    act.wait_ge(raw_in[slot_of(section)][q], 16 * lap_of(section))
            for kh in range(2):
                act.wait_ge(s.pieces_used, blk * 2 + (PIECES * section + kh + 1))
                b = 2 * odd + kh
                act.copy(whi[:, b, :].rearrange("p (k c) -> p k c", c=P), piece(section, blk, kh)).then_inc(s.hi_ready, 1)

        def evacuate(section, blk, odd):
            if section in (WM, WA):
                return
            act.wait_ge(s.pieces_used, blk * 2 + (PIECES * section + 2 + NBUF))
            src = ps[:, bank(section, odd), :]
            b1 = bass.ds(blk, 1)
            if section == XM:
                act.copy(xm[:, b1, CONV - 1:], src[:, 0:S].unsqueeze(1)).then_inc(evac[XM], 1)
            elif section == OG:
                act.activation(ot[:, b1, :], src[:, 0:T].unsqueeze(1), ACT.Sigmoid).then_inc(evac[OG], 1)
            elif section == KA:
                act.copy(ka[:, b1, :], src[:, 0:S].unsqueeze(1)).then_inc(evac[KA], 1)
            elif section == QA:
                act.mul(qa[0:AD, 0, b1, :], src[0:AD, 0:T].unsqueeze(1), AD ** -0.5)
                act.mul(qa[AD:P, 1, b1, :], src[AD:P, 0:T].unsqueeze(1), AD ** -0.5).then_inc(evac[QA], 1)
            elif section == VA:
                act.copy(vat[:, b1, :], src[:, 0:S].unsqueeze(1)).then_inc(evac[VA], 1)
            else:
                act.activation(sg[:, b1, :], src[:, 0:T].unsqueeze(1), ACT.Sigmoid).then_inc(evac[section], 1)

        def stream(section, following, extra=None):
            with act.Fori(0, KB // 2 - 1) as i:
                for j in range(2):
                    split(section, i * 2 + (j + 1), (j + 1) % 2)
                    evacuate(section, i * 2 + j, j)
                    if extra:
                        extra(i * 2 + j, j)
            split(section, KB - 1, 1)
            evacuate(section, KB - 2, 0)
            if extra:
                extra(KB - 2, 0)
            if following is not None:
                split(following, 0, 0)
            evacuate(section, KB - 1, 1)
            if extra:
                extra(KB - 1, 1)

        def conv_sigmoid(blk, odd):
            act.wait_ge(s.conv_acc, blk + 1)
            act.wait_ge(s.xc_ready, blk + 1)
            act.activation(csig[:, odd, :], xc[:, bass.ds(blk, 1), :], ACT.Sigmoid).then_inc(s.conv_sig, 1)

        split(XM, 0, 0)
        stream(XM, OG)
        act.wait_ge(s.hres_ready, 1)
        stream(OG, None, conv_sigmoid)

        for g in range(16):
            act.wait_ge(s.hp_done, g + 1)
            if g % 2 == 0:
                act.copy(qm[:, g // 2, :], ps[:, 4 + g % 4, 0:T]).then_inc(s.hp_act, 1)
            else:
                act.mul(km[:, g // 2, :], ps[:, 4 + g % 4, 0:S], MD ** -0.5).then_inc(s.hp_act, 1)
            if g == 3:
                act.wait_ge(s.scan_e, 1)
                act.activation(scan[:, 1, SCAN:], gtmp[:, 1, :], ACT.Exp, scale=-1.0).then_inc(s.act, 1)
                act.wait_ge(s.act, 1)
                act.activation(gtmp[:, 1, :], scan[:, 1, SCAN:], ACT.Ln, bias=1.0).then_inc(s.scan_l, 1)
        act.wait_ge(s.vm_ones, 1)
        for g in range(16, 28):
            h, st = divmod(g - 16, 3)
            n = STILES[st][1]
            act.wait_ge(s.hp_done, g + 1)
            act.copy(vm[0:n, st, h, 0:MD], ps[0:n, 4 + g % 4, 0:MD]).then_inc(s.hp_act, 1)
        act.wait_ge(s.aux_ready, 2)
        act.activation(em_col[:], ps[:, 7, 12:20].rearrange("p (t h) -> p t h", h=MH), ACT.Exp).then_inc(s.exp_ready, 1)
        act.wait_ge(s.aux_ready, 2)
        for h in range(MH):
            act.wait_ge(s.mb_done, h + 1)
            if h >= 2:
                act.wait_ge(s.w_done, h - 1)
            for (c0, n, rows), st in zip(((0, 256, P), (256, 144, P), (400, META, META)), range(3)):
                last = act.activation(ex[0:rows, h % 2, c0:c0 + n], ps[0:rows, 4 + h % 2, c0:c0 + n], ACT.Exp,
                                      bias=at_col[0:rows, st, h:h + 1], scale=-1.0)
            last.then_inc(s.e_done, 1)

        act.wait_ge(s.num_done, MH)
        act.wait_ge(s.qa_zero, 2)
        split(KA, 0, 0)
        stream(KA, QA)
        stream(QA, VA)
        stream(VA, None)

        for g in range(6):
            st, half = divmod(g, 2)
            n = STILES[st][1]
            act.wait_ge(s.va_t, g + 1)
            act.copy(va[0:n, st, 512 * half:512 * half + 512], ps[0:n, 4 + g % 4, :]).then_inc(s.va_ready, 1)

        def softmax_exp(h):
            act.wait_ge(s.nmax_done, h + 1)
            if h >= 2:
                act.wait_ge(s.tr_done, h - 1)
            for t, (c0, n) in enumerate(((0, 144), (144, S))):
                for half in range(2):
                    last = act.activation(ea[:, h % 2, half, c0:c0 + n], ps[:, 4 + 2 * (h % 2) + half, c0:c0 + n],
                                          ACT.Exp, bias=nmax[:, h % 2, t, half:half + 1],
                                          accum_out=rsum[:, h % 2, t, half:half + 1])
            last.then_inc(s.exp_done, 1)

        softmax_exp(0)
        for h in range(AH):
            if h + 1 < AH:
                softmax_exp(h + 1)
            act.wait_ge(s.tr_done, h + 1)
            if h >= 1:
                act.wait_ge(s.av_done, h)
            act.copy(att[:], ps[:, 0, 0:3 * P]).then_inc(s.at_act, 1)
            act.wait_ge(s.o_copied, h + 1)
            if h:
                act.wait_ge(s.o_squared, TT * h)
            for t in range(TT):
                act.activation(junk[t][:], oall[:, t, P * h:P * h + P], ACT.Square,
                               accum_out=ssq[:, t * AH + h:t * AH + h + 1]).then_inc(s.o_squared, 1)

        split(GA, 0, 0)
        stream(GA, None)
        for k in range(KB):
            act.wait_ge(s.ym_full, k + 1)
            act.copy(ym_hi[:, k, :], mtmp[:, k % 2, :]).then_inc(s.ym_hi_s, 1)
        for k in range(KB):
            act.wait_ge(s.ya_full, k + 1)
            act.copy(ya_hi[:, k, :], mtmp[:, k % 2, :]).then_inc(s.ya_hi_s, 1)
        for j, v in enumerate((ln1_g, ln1_b)):
            act.dma_start(rows1[:, j, :], v[0].partition_broadcast(P)).then_inc(s.rows1_in, 16)
        split(WM, 0, 0)
        stream(WM, GB)
        act.wait_ge(evac[WM], KB + 2)
        stream(GB, WA)
        stream(WA, None)
        for n in range(PIECES):
            if n == 0:
                for q in range(4):
                    act.wait_ge(raw_in[slot_of("out")][q], 16 * lap_of("out"))
            if n == NBUF:
                for half in range(2):
                    act.wait_ge(s.merged_s, 1)
                    act.copy(mg_hi[:, 4 * half:4 * half + 4, :], merged[:, 4 * half:4 * half + 4, :]).then_inc(s.mg_hi_s, 1)
            act.wait_ge(s.pieces_used, OUT_BASE + n + 1)
            act.copy(whi[:, n % NBUF, :], out_piece(n)).then_inc(s.hi_ready, 1)

        for t in range(TT):
            act.wait_ge(s.h1_ready, t + 1)
            act.mul(acc[:, t, :], h1[:, t, :], ALPHA).then_inc(s.acc_ready, 1)
        for half in range(2):
            act.wait_ge(s.h1_t, 2 * half + 1)
            act.copy(h1t[:, 0:4, P * half:P * half + P], ps[:, 2 * half, :].rearrange("p (k c) -> p k c", c=P)).then_inc(s.h1t_act, 1)
        act.wait_ge(s.logit_done, 1)
        act.copy(lgt[:], ps[0:NE, 4, 0:T]).then_inc(s.logit_sb, 1)
        act.wait_ge(s.h1_ready, TT)
        for j, v in enumerate((ln2_g, ln2_b)):
            act.dma_start(rows1[:, j, :], v[0].partition_broadcast(P)).then_inc(s.rows2_in, 16)
        act.wait_ge(s.router_exp, 1)
        for t in range(TT):
            act.activation(rt[:, 1, NE * t:NE * t + NE], rt[:, 0, NE * t:NE * t + NE], ACT.Exp,
                           bias=rt[:, 15, t:t + 1]).then_inc(s.exp_r, 1)

        act.wait_ge(s.units_ready, 1)
        with act.Fori(0, NE) as e:
            nb = act.value_load(units[0:1, 0, bass.ds(e, 1)], min_val=1, max_val=MAXBLK)
            first = act.value_load(units[0:1, 1, bass.ds(e, 1)], min_val=0, max_val=NE * MAXBLK)
            with act.Fori(0, nb) as b:
                u = act.snap(first + b)
                for half in range(2):
                    act.wait_ge(s.gate_used, u * 4 + 4)
                    act.copy(gsb[:, 512 * half:512 * half + 512], ps[:, half, :]).then_inc(s.gsb_ready, 1)
                act.wait_ge(s.gate_ready, u + 1)
                act.activation(gsig[:], gate[:], ACT.Sigmoid).then_inc(s.gsig_ready, 1)
                for half in range(2):
                    act.wait_ge(s.up_used, u * 4 + 4)
                    act.copy(usb[:, 512 * half:512 * half + 512], ps[:, 2 + half, :]).then_inc(s.usb_ready, 1)
                for half in range(2):
                    act.wait_ge(s.down_used, u * 4 + 4)
                    act.copy(zsb[:, 512 * half:512 * half + 512], ps[:, 6 + half, :]).then_inc(s.z_ready, 1)

    @block.vector
    def _(dve):
        own = Steps(dve, s.dve)
        for j, n in enumerate((META, P, P)):
            dve.wait_ge((s.x_in0, s.x_in1, s.x_in2)[j], 16)
            for c in range(2):
                own(dve.bn_stats(stats[0:n, j, c, :], xt[0:n, j, 512 * c:512 * c + 512]))
        own.settle()
        for j, n in enumerate((META, P, P)):
            own(dve.bn_aggr(mv[0:n, j, :], stats[0:n, j, :, :]))
        own.settle()
        for j, n in enumerate((META, P, P)):
            dve.tensor_scalar(ve[0:n, j:j + 1], mv[0:n, j, 1:2], EPS, None, ALU.add).then_inc(s.var_ready, 1)
        dve.wait_ge(s.lam_in, 64)
        own(dve.tensor_tensor(lamp[:], lamv[:, 0:2, :], lamv[:, 2:4, :], ALU.mult))
        own.settle()
        dve.tensor_reduce(lams[:, 0:2], lamp[:], AX.X, ALU.add).then_inc(s.lam_sum, 1)
        dve.wait_ge(s.rstd_ready, 2)
        for j, n in enumerate((META, P, P)):
            dve.tensor_scalar(xt[0:n, j, :], xt[0:n, j, :], mv[0:n, j, 0:1], rstd[0:n, j:j + 1],
                              ALU.subtract, ALU.mult).then_inc(s.xn_ready, 1)
        dve.wait_ge(s.rows_t, 1)
        dve.tensor_copy(chan[:], ps[:, 7, 0:65]).then_inc(s.chan_ready, 1)
        dve.wait_ge(s.chan_ready, 1)
        own(dve.tensor_scalar(chan[:, C_AG:C_AG + 1], chan[:, C_AG:C_AG + 1], 1.0 - LAM_INIT, None, ALU.mult))
        dve.wait_ge(s.lam_exp, 1)
        own(dve.tensor_tensor(neglam[:], lams[:, 3:4], lams[:, 2:3], ALU.subtract))
        own.settle()
        own(dve.tensor_scalar(neglam[:], neglam[:], -LAM_INIT, None, ALU.add))

        def low_half(k):
            dve.wait_ge(s.h_hi, k + 1)
            dve.tensor_tensor(lo_h[:, k, :], hfull[:, k % 2, :], hi_h[:, k, :].bitcast(F32),
                              ALU.subtract).then_inc(s.h_lo, 1)

        for k in range(KB):
            dve.wait_ge(s.ht_t, k + 1)
            if k >= 2:
                dve.wait_ge(s.h_lo, k - 1)
            dve.tensor_scalar(hfull[:, k % 2, :], ps[:, k % 4, 0:S], chan[:, C_LNG + k:C_LNG + k + 1],
                              chan[:, C_LNB + k:C_LNB + k + 1], ALU.mult, ALU.add).then_inc(s.h_full, 1)
            if k:
                low_half(k - 1)
        low_half(KB - 1)
        dve.wait_ge(s.wif_split, 2)
        for a, b in ((0, MH), (32, 0)):
            own(dve.tensor_tensor(wif_lo[:, :, a:a + MH], wif[:, :, b:b + MH],
                                  wif_hi[:, :, a:a + MH].bitcast(F32), ALU.subtract))
        own.settle()
        dve.sem_inc(s.wif_split, 1)

        def split(section, blk, odd):
            for kh in range(2):
                b = 2 * odd + kh
                dve.wait_ge(s.hi_ready, blk * 2 + (PIECES * section + kh + 1))
                dve.tensor_tensor(wlo[:, b, :].rearrange("p (k c) -> p k c", c=P), piece(section, blk, kh),
                                  whi[:, b, :].bitcast(F32).rearrange("p (k c) -> p k c", c=P),
                                  ALU.subtract).then_inc(s.lo_ready, 1)

        def evacuate(section, blk, odd):
            if section not in (WM, WA):
                return
            dve.wait_ge(s.pieces_used, blk * 2 + (PIECES * section + 2 + NBUF))
            src = ps[:, bank(section, odd), 0:T].unsqueeze(1)
            b1 = bass.ds(blk, 1)
            if section == WM:
                dve.tensor_tensor(merged[:, b1, :], src, sg[:, b1, :], ALU.mult).then_inc(evac[WM], 1)
            else:
                own.settle()
                dve.tensor_tensor(mtmp[:, odd:odd + 1, :], src, sg[:, b1, :], ALU.mult).then_inc(evac[WA], 1)
                dve.wait_ge(evac[WA], blk + 3)
                own(dve.tensor_tensor(merged[:, b1, :], mtmp[:, odd:odd + 1, :], merged[:, b1, :], ALU.add))

        def stream(section, following, extra=None, per=0):
            n0 = own.n
            with dve.Fori(0, KB // 2 - 1) as i:
                own.base = i * (2 * per)
                for j in range(2):
                    split(section, i * 2 + (j + 1), (j + 1) % 2)
                    evacuate(section, i * 2 + j, j)
                    if extra:
                        extra(i * 2 + j, j)
            assert own.n == n0 + 2 * per
            own.base = 0
            own.n = n0 + (KB - 2) * per
            split(section, KB - 1, 1)
            evacuate(section, KB - 2, 0)
            if extra:
                extra(KB - 2, 0)
            if following is not None:
                split(following, 0, 0)
            evacuate(section, KB - 1, 1)
            if extra:
                extra(KB - 1, 1)

        def conv(blk, odd):
            b1 = bass.ds(blk, 1)
            if isinstance(blk, int):
                cols = [c_conv(w, blk) for w in range(CONV)] + [chan[:, C_CONVB + blk:C_CONVB + blk + 1]]
            else:
                cols = [c_conv(w, blk) for w in range(CONV)] + [chan[:, bass.ds(blk + C_CONVB, 1)]]
            own(dve.tensor_scalar(xc[:, b1, :], xm[:, b1, 0:S], cols[0], cols[CONV], ALU.mult, ALU.add))
            for w in range(1, CONV):
                own.settle()
                ins = dve.scalar_tensor_tensor(out=xc[:, b1, :], in0=xm[:, b1, w:w + S], scalar=cols[w],
                                               in1=xc[:, b1, :], op0=ALU.mult, op1=ALU.add)
                if w < CONV - 1:
                    own(ins)
                else:
                    ins.then_inc(s.conv_acc, 1)

        split(XM, 0, 0)
        stream(XM, OG)
        dve.wait_ge(evac[XM], KB + 2)
        stream(OG, None, conv, per=CONV - 1)

        dve.wait_ge(s.gb_in, 32)
        dve.wait_ge(s.if_done, 1)
        own(dve.memset(scan[:, :, 0:SCAN], 0.0))
        own(dve.tensor_scalar(gtmp[:, 0, :], ps[0:MH, 0, 0:S], gate_bias[:, 1:2], None, ALU.add))
        own(dve.tensor_copy(scan[:, 2, SCAN:], ps[32:32 + MH, 0, 0:S]))
        own.settle()
        dve.scalar_tensor_tensor(out=gtmp[:, 1, :], in0=gtmp[:, 0, :], scalar=-1.0, in1=gtmp[:, 0, :],
                                 op0=ALU.mult, op1=ALU.max).then_inc(s.scan_e, 1)
        own(dve.tensor_scalar(gtmp[:, 0, :], gtmp[:, 0, :], 0.0, None, ALU.min))
        dve.wait_ge(s.scan_l, 1)
        own.settle()
        own(dve.tensor_tensor(scan[:, 0, SCAN:], gtmp[:, 0, :], gtmp[:, 1, :], ALU.subtract))
        own.settle()

        def prefix(src, dst, op):
            step = 1
            while step < S:
                own(dve.tensor_tensor(scan[:, dst, SCAN:], scan[:, src, SCAN:],
                                      scan[:, src, SCAN - step:SCAN - step + S], op))
                own.settle()
                src, dst, step = dst, src, 2 * step
            return src

        b_at = prefix(0, 1, ALU.add)
        own(dve.scalar_tensor_tensor(out=gtmp[:, 0, :], in0=scan[:, 2, SCAN:], scalar=gate_bias[:, 0:1],
                                     in1=scan[:, b_at, SCAN:], op0=ALU.add, op1=ALU.subtract))
        own.settle()
        own(dve.tensor_copy(scan[:, 2, SCAN:], gtmp[:, 0, :]))
        own.settle()
        m_at = prefix(2, 1 - b_at, ALU.max)
        own(dve.tensor_scalar(mrow[:], scan[:, m_at, SCAN:], 0.0, None, ALU.max))
        own.settle()
        dve.scalar_tensor_tensor(out=gtmp[:, 1, :], in0=scan[:, b_at, SCAN:], scalar=-1.0, in1=mrow[:],
                                 op0=ALU.mult, op1=ALU.subtract).then_inc(s.gates_ready, 1)
        dve.wait_ge(s.gates_t, 1)
        dve.tensor_copy(at_col[:, 0:2, :], ps[:, 7, 0:8].rearrange("p (t h) -> p t h", h=MH)).then_inc(s.aux_ready, 1)
        dve.tensor_copy(at_col[0:META, 2, :], ps[0:META, 7, 8:12]).then_inc(s.aux_ready, 1)
        for g in range(4):
            t, half = divmod(g, 2)
            dve.wait_ge(s.ot_t, g + 1)
            dve.tensor_copy(hh[:, t, 512 * half:512 * half + 512], ps[:, g, :]).then_inc(s.ot_ready, 1)

        def weights(h):
            dve.wait_ge(s.e_done, h + 1)
            dve.wait_ge(s.sc_done, h + 1)
            if h == 0:
                dve.wait_ge(s.vm_ones, 5)
            if h >= 2:
                dve.wait_ge(s.num_done, h - 1)
            b, e = 6 + h % 2, h % 2
            own(dve.tensor_tensor(wgt[:, e, 0, :], ps[:, b, 0:256], ex[:, e, 0:256], ALU.mult))
            own(dve.tensor_tensor(wgt[:, e, 1, 112:256], ps[:, b, 256:400], ex[:, e, 256:400], ALU.mult))
            dve.tensor_tensor(wgt[0:META, e, 2, 240:256], ps[0:META, b, 400:416], ex[0:META, e, 400:416],
                              ALU.mult).then_inc(s.w_done, 1)

        def outputs(h):
            dve.wait_ge(s.num_done, h + 1)
            dve.wait_ge(s.exp_ready, 1)
            for t in range(TT):
                own(dve.tensor_scalar(den[:, h, t:t + 1], ps[:, 2 * (h % 2) + t, MD:MD + 1], -1.0,
                                      em_col[:, t, h:h + 1], ALU.mult, ALU.max))
            own.settle()
            for t in range(TT):
                own(dve.tensor_tensor(den[:, h, t:t + 1], ps[:, 2 * (h % 2) + t, MD:MD + 1], den[:, h, t:t + 1],
                                      ALU.max))
            own.settle()
            own(dve.reciprocal(rden[:, h, :], den[:, h, :]))
            own.settle()
            for t in range(TT):
                cols = slice(MD * h, MD * h + MD)
                dve.scalar_tensor_tensor(out=hh[:, t, cols], in0=ps[:, 2 * (h % 2) + t, 0:MD],
                                         scalar=rden[:, h, t:t + 1], in1=hh[:, t, cols],
                                         op0=ALU.mult, op1=ALU.mult).then_inc(s.hh_done, 1)

        dve.wait_ge(s.ot_ready, 4)
        weights(0)
        for h in range(MH):
            if h + 1 < MH:
                weights(h + 1)
            outputs(h)
        dve.wait_ge(s.hh_done, TT * MH)
        for i in range(TT * MH):
            t, h = divmod(i, MH)
            own(dve.bn_stats(stats8[:, i, :], hh[:, t, MD * h:MD * h + MD]))
        own.settle()
        for i in range(TT * MH):
            own(dve.bn_aggr(mv8[:, i, :], stats8[:, i, :]))
        own.settle()
        dve.tensor_scalar(ve8[:], mv8[:, :, 1], EPS, None, ALU.add).then_inc(s.var8, 1)
        dve.wait_ge(s.rstd8_ready, 1)
        for i in range(TT * MH):
            t, h = divmod(i, MH)
            cols = slice(MD * h, MD * h + MD)
            dve.tensor_scalar(hh[:, t, cols], hh[:, t, cols], mv8[:, i, 0:1], rstd8[:, i:i + 1],
                              ALU.subtract, ALU.mult).then_inc(s.hn_ready, 1)

        split(KA, 0, 0)
        stream(KA, QA)
        stream(QA, VA)
        stream(VA, None)

        def row_max(h):
            dve.wait_ge(s.s_done, h + 1)
            b = 4 + 2 * (h % 2)
            for t, (c0, n) in enumerate(((0, 144), (144, S))):
                last = dve.tensor_reduce(nmax[:, h % 2, t, :], ps[:, b:b + 2, c0:c0 + n], AX.X, ALU.max, negate=True)
            last.then_inc(s.nmax_done, 1)

        def combine(h):
            e = h % 2
            dve.wait_ge(s.exp_done, h + 1)
            own(dve.reciprocal(rinv[:, e, :, :], rsum[:, e, :, :]))
            own.settle()
            own(dve.tensor_scalar(rinv[:, e, :, 1], rinv[:, e, :, 1], neglam[:, 0:1], None, ALU.mult))
            for t, (c0, n) in enumerate(((0, 144), (144, S))):
                own(dve.tensor_scalar(ea[:, e, 0, c0:c0 + n], ea[:, e, 0, c0:c0 + n], rinv[:, e, t, 0:1], None, ALU.mult))
            own.settle()
            for t, (c0, n) in enumerate(((0, 144), (144, S))):
                ins = dve.scalar_tensor_tensor(out=ea[:, e, 0, c0:c0 + n], in0=ea[:, e, 1, c0:c0 + n],
                                               scalar=rinv[:, e, t, 1:2], in1=ea[:, e, 0, c0:c0 + n],
                                               op0=ALU.mult, op1=ALU.add)
                if t:
                    ins.then_inc(s.attn_done, 1)
                else:
                    own(ins)

        row_max(0)
        for h in range(AH):
            if h + 1 < AH:
                row_max(h + 1)
            combine(h)
            dve.wait_ge(s.tr_done, h + 1)
            if h >= 1:
                dve.wait_ge(s.av_done, h)
            dve.tensor_copy(att2[:], ps[0:META, 1, 0:2 * P]).then_inc(s.at_dve, 1)
            dve.wait_ge(s.av_done, h + 1)
            dve.tensor_copy(oall[:, :, P * h:P * h + P],
                            ps[:, 2 + h % 2, 0:2 * P].rearrange("p (t v) -> p t v", v=P)).then_inc(s.o_copied, 1)
        dve.wait_ge(s.o_squared, TT * AH)
        dve.tensor_scalar(vea[:], ssq[:], 1.0 / AV, EPS, ALU.mult, ALU.add).then_inc(s.vara, 1)
        dve.wait_ge(s.rstda_ready, 1)
        dve.wait_ge(s.o_copied, AH)
        o4 = oall[:].rearrange("p t (h v) -> p (t h) v", v=AV)
        dve.tensor_tensor(o4, o4, rstda[:].unsqueeze(2).to_broadcast([P, TT * AH, AV]), ALU.mult).then_inc(s.ya_ready, 1)

        split(GA, 0, 0)
        stream(GA, None)
        def branch(turned, full, hi_sem, lo_sem, hi, lo, gain, before_sem):

            def low(k):
                dve.wait_ge(hi_sem, k + 1)
                dve.tensor_tensor(lo[:, k, :], mtmp[:, k % 2, :], hi[:, k, :].bitcast(F32),
                                  ALU.subtract).then_inc(lo_sem, 1)

            if before_sem is not None:
                dve.wait_ge(before_sem, KB)
            for k in range(KB):
                dve.wait_ge(turned, k // 2 + 1)
                if k >= 2:
                    dve.wait_ge(lo_sem, k - 1)
                dve.tensor_scalar(mtmp[:, k % 2, :], ps[:, 4 + k // 2, T * (k % 2):T * (k % 2) + T], gain(k), None,
                                  ALU.mult).then_inc(full, 1)
                if k:
                    low(k - 1)
            low(KB - 1)

        branch(s.ym_t, s.ym_full, s.ym_hi_s, s.ym_lo_s, ym_hi, ym_lo, lambda k: chan[:, C_MG + k:C_MG + k + 1], None)
        branch(s.ya_t, s.ya_full, s.ya_hi_s, s.ya_lo_s, ya_hi, ya_lo, lambda k: chan[:, C_AG:C_AG + 1], s.ym_lo_s)
        split(WM, 0, 0)
        stream(WM, GB)
        stream(GB, WA)
        stream(WA, None, per=1)
        own.settle()
        dve.sem_inc(s.merged_s, 1)
        for n in range(PIECES):
            if n == NBUF:
                for half in range(2):
                    dve.wait_ge(s.mg_hi_s, half + 1)
                    c = slice(4 * half, 4 * half + 4)
                    dve.tensor_tensor(mg_lo[:, c, :], merged[:, c, :], mg_hi[:, c, :].bitcast(F32),
                                      ALU.subtract).then_inc(s.mg_lo_s, 1)
            dve.wait_ge(s.hi_ready, OUT_BASE + n + 1)
            dve.tensor_tensor(wlo[:, n % NBUF, :], out_piece(n), whi[:, n % NBUF, :].bitcast(F32),
                              ALU.subtract).then_inc(s.lo_ready, 1)

        def norm(done_var, rstd_sem, buf, rows_sem, ready):
            for t in range(TT):
                for c in range(2):
                    own(dve.bn_stats(stats[:, t, c, :], buf[:, t, 512 * c:512 * c + 512]))
            own.settle()
            for t in range(TT):
                own(dve.bn_aggr(mv[:, t, :], stats[:, t, :, :]))
            own.settle()
            dve.tensor_scalar(ve[:, 0:TT], mv[:, 0:TT, 1], EPS, None, ALU.add).then_inc(done_var, 1)
            dve.wait_ge(rstd_sem, 1)
            for t in range(TT):
                own(dve.tensor_scalar(buf[:, t, :], buf[:, t, :], mv[:, t, 0:1], rstd[:, t:t + 1],
                                      ALU.subtract, ALU.mult))
            own.settle()
            dve.wait_ge(rows_sem, 32)
            for t in range(TT):
                own(dve.tensor_tensor(buf[:, t, :], buf[:, t, :], rows1[:, 0, :], ALU.mult))
                own.settle()
                dve.tensor_tensor(buf[:, t, :], buf[:, t, :], rows1[:, 1, :], ALU.add).then_inc(ready, 1)

        dve.wait_ge(s.pieces_used, OUT_BASE + PIECES + NBUF)
        dve.wait_ge(s.hres_ready, 1)
        for t in range(TT):
            for c in range(2):
                last = dve.scalar_tensor_tensor(out=h1[:, t, 512 * c:512 * c + 512],
                                                in0=hres[:, t, 512 * c:512 * c + 512], scalar=ALPHA,
                                                in1=ps[:, 4 + 2 * t + c, :], op0=ALU.mult, op1=ALU.add)
        last.then_inc(s.resid_done, 1)
        dve.wait_ge(s.resid_done, 1)
        norm(s.var1, s.rstd1, h1, s.rows1_in, s.h1_ready)
        for half in range(2):
            dve.wait_ge(s.h1_t, 2 * half + 2)
            dve.tensor_copy(h1t[:, 4:8, P * half:P * half + P],
                            ps[:, 2 * half + 1, :].rearrange("p (k c) -> p k c", c=P)).then_inc(s.h1t_dve, 1)

        def val(r):
            return rt[:, r, :].rearrange("p (t e) -> p t e", e=NE)

        def grp(r):
            return rt[:, r, :].rearrange("p (t g i) -> p t g i", g=NG, i=EPG)

        def first_max(src, r_eq, r_key, r_one, out_row, groups):
            n = NG if groups else NE
            rank = rank16[:, NE - n:NE].unsqueeze(1).to_broadcast([P, TT, n])
            own(dve.tensor_reduce(r_one, src, AX.X, ALU.max))
            own.settle()
            own(dve.tensor_tensor(r_eq, src, r_one.unsqueeze(2).to_broadcast([P, TT, n]), ALU.is_equal))
            own.settle()
            own(dve.tensor_tensor(r_key, r_eq, rank, ALU.mult))
            own.settle()
            own(dve.tensor_reduce(r_one, r_key, AX.X, ALU.max))
            own.settle()
            own(dve.tensor_tensor(out_row, r_key, r_one.unsqueeze(2).to_broadcast([P, TT, n]), ALU.is_equal))
            own.settle()

        dve.wait_ge(s.logit_t, 1)
        own(dve.tensor_copy(val(0), ps[:, 5, 0:TT * NE].rearrange("p (t e) -> p t e", e=NE)))
        own.settle()
        dve.tensor_reduce(rt[:, 15, 0:TT], val(0), AX.X, ALU.max, negate=True).then_inc(s.router_exp, 1)
        dve.wait_ge(s.exp_r, TT)
        own(dve.tensor_reduce(rt[:, 15, 4:4 + TT], val(1), AX.X, ALU.add))
        own.settle()
        own(dve.reciprocal(rt[:, 15, 8:8 + TT], rt[:, 15, 4:4 + TT]))
        own.settle()
        own(dve.tensor_tensor(val(2), val(1), rt[:, 15, 8:8 + TT].unsqueeze(2).to_broadcast([P, TT, NE]), ALU.mult))
        own.settle()
        dve.wait_ge(s.rb_in, 16)
        own(dve.tensor_tensor(val(3), val(2), rbias[:].unsqueeze(1).to_broadcast([P, TT, NE]), ALU.add))
        own.settle()
        g8 = rt[:, 4, 0:TT * NG].rearrange("p (t g) -> p t g", g=NG)
        e8 = rt[:, 5, 0:TT * NG].rearrange("p (t g) -> p t g", g=NG)
        k8 = rt[:, 6, 0:TT * NG].rearrange("p (t g) -> p t g", g=NG)
        own(dve.tensor_reduce(g8, grp(3), AX.X, ALU.max))
        own.settle()
        first_max(g8, e8, k8, rt[:, 15, 12:12 + TT], g8, True)
        own(dve.tensor_scalar(g8, g8, BIG, -BIG, ALU.mult, ALU.add))
        own.settle()
        own(dve.tensor_tensor(grp(3), grp(3), rt[:, 4, 0:TT * NG].rearrange("p (t g) -> p t g", g=NG).unsqueeze(3)
                              .to_broadcast([P, TT, NG, EPG]), ALU.add))
        own.settle()
        first_max(val(3), val(5), val(6), rt[:, 15, 16:16 + TT], val(7), False)
        own(dve.scalar_tensor_tensor(out=val(3), in0=val(7), scalar=-3.0 * BIG, in1=val(3), op0=ALU.mult, op1=ALU.add))
        own.settle()
        first_max(val(3), val(5), val(6), rt[:, 15, 20:20 + TT], val(8), False)
        dve.tensor_tensor(mask[:], val(7), val(8), ALU.add).then_inc(s.mask_ready, 1)
        dve.wait_ge(s.mask_ready, 1)
        own(dve.tensor_tensor(val(9), mask[:], val(2), ALU.mult))
        own.settle()
        own(dve.tensor_reduce(rt[:, 15, 24:24 + TT], val(9), AX.X, ALU.add))
        own.settle()
        own(dve.reciprocal(rt[:, 15, 28:28 + TT], rt[:, 15, 24:24 + TT]))
        own.settle()
        own(dve.tensor_tensor(comb[:], val(9), rt[:, 15, 28:28 + TT].unsqueeze(2).to_broadcast([P, TT, NE]), ALU.mult))
        dve.wait_ge(s.rank_done, 1)
        own(dve.scalar_tensor_tensor(out=slot[:], in0=ps[:, 6, 0:TT * NE].rearrange("p (t e) -> p t e", e=NE),
                                     scalar=1.0, in1=mask[:], op0=ALU.add, op1=ALU.mult))
        own(dve.tensor_copy(counts[:], ps[0:1, 6, 2 * NE:3 * NE]))
        own.settle()
        own(dve.tensor_scalar(slot[:], slot[:], -1.0, None, ALU.add))
        own(dve.tensor_scalar(nblk_f[:], counts[:], float(SLOTS), 1.0, ALU.is_gt, ALU.add))
        own.settle()
        for c in (2, 3):
            own(dve.scalar_tensor_tensor(out=nblk_f[:], in0=counts[:], scalar=float(c * SLOTS), in1=nblk_f[:],
                                         op0=ALU.is_gt, op1=ALU.add))
            own.settle()
        own(dve.memset(ends_f[:], 0.0))
        own.settle()
        own(dve.tensor_copy(ends_f[:, 0, 32:], nblk_f[:]))
        own.settle()
        src = 0
        for step in (1, 2, 4, 8):
            own(dve.tensor_tensor(ends_f[:, 1 - src, 32:], ends_f[:, src, 32:], ends_f[:, src, 32 - step:32 - step + NE],
                                  ALU.add))
            own.settle()
            src = 1 - src
        own(dve.tensor_copy(units[:, 0, :], nblk_f[:]))
        own(dve.tensor_tensor(ends_f[:, 1 - src, 32:], ends_f[:, src, 32:], nblk_f[:], ALU.subtract))
        own(dve.tensor_scalar(units[:, 2, :], ends_f[:, src, 32:], -1.0, None, ALU.add))
        own.settle()
        dve.tensor_copy(units[:, 1, :], ends_f[:, 1 - src, 32:]).then_inc(s.units_ready, 1)
        dve.wait_ge(s.units_ready, 1)

        dve.wait_ge(s.acc_ready, TT)
        with dve.Fori(0, NE) as e:
            nb = dve.value_load(units[0:1, 0, bass.ds(e, 1)], min_val=1, max_val=MAXBLK)
            first = dve.value_load(units[0:1, 1, bass.ds(e, 1)], min_val=0, max_val=NE * MAXBLK)
            with dve.Fori(0, nb) as b:
                u = dve.snap(first + b)
                for t in range(TT):
                    dve.tensor_scalar(pick[:, t, :], slotno[:].rearrange("p a b -> p (a b)"), boff[:, bass.ds(b, 1)],
                                      slot[:, t, bass.ds(e, 1)], ALU.add, ALU.is_equal).then_inc(s.pick_ready, 1)
                dve.wait_ge(s.pick_ready, u * 2 + 2)
                for t in range(TT):
                    dve.tensor_scalar(wpick[:, t, :], pick[:, t, :], comb[:, t, bass.ds(e, 1)], None,
                                      ALU.mult).then_inc(s.wpick_ready, 1)
                dve.wait_ge(s.gath_done, u + 1)
                dve.tensor_copy(xg[:], ps[:, 4:6, :].rearrange("p a (k c) -> p (a k) c", c=P)[:, :, 0:SLOTS]
                                ).then_inc(s.xg_ready, 1)
                dve.wait_ge(s.tg_done, u + 1)
                dve.tensor_reduce(gate[:], ps[:, 4:6, :].rearrange("p a (k h s) -> p (a k) s h", h=2, s=SLOTS), AX.X,
                                  ALU.add).then_inc(s.gate_ready, 1)
                dve.wait_ge(s.gsig_ready, u + 1)
                dve.wait_ge(s.gate_ready, u + 1)
                dve.tensor_tensor(gate[:], gate[:], gsig[:], ALU.mult).then_inc(s.moe_dve, 1)
                dve.wait_ge(s.tu_done, u + 1)
                dve.tensor_reduce(upv[:], ps[:, 0:2, :].rearrange("p a (k h s) -> p (a k) s h", h=2, s=SLOTS), AX.X,
                                  ALU.add).then_inc(s.moe_dve, 1)
                dve.wait_ge(s.moe_dve, u * 2 + 2)
                dve.tensor_tensor(hid[:], gate[:], upv[:], ALU.mult).then_inc(s.hid_ready, 1)
                for j in range(4):
                    t, c = divmod(j, 2)
                    cols = slice(512 * c, 512 * c + 512)
                    dve.wait_ge(s.scat_done, u * 4 + (j + 1))
                    dve.tensor_tensor(acc[:, t, cols], ps[:, 2 + j, :], acc[:, t, cols], ALU.add).then_inc(s.acc_added, 1)
                dve.wait_ge(s.wpt_t, u + 1)
                dve.tensor_copy(wpt[:], ps[:, 0, 0:2 * P].rearrange("p (t c) -> p t c", c=P)).then_inc(s.wpt_ready, 1)
        end = dve.value_load(units[0:1, 2, NE - 1:NE], min_val=0, max_val=NE * MAXBLK)
        for j in range(4):
            t, c = divmod(j, 2)
            cols = slice(512 * c, 512 * c + 512)
            dve.wait_ge(s.scat_done, end * 4 + (j + 5))
            dve.tensor_tensor(acc[:, t, cols], ps[:, 2 + j, :], acc[:, t, cols], ALU.add).then_inc(s.acc_added, 1)
        dve.wait_ge(s.acc_added, end * 4 + 12)
        norm(s.fin_var, s.fin_rstd, acc, s.rows2_in, s.fin_ready)

    @block.tensor
    def _(pe):
        mm = pe.matmul
        pe.sem_inc(s.pieces_used, NBUF)
        pe.wait_ge(s.consts, 1)
        pe.wait_ge(s.crow_in, 96)
        pe.transpose(ps[:, 7, 0:65], crow[:], ident[0:65, 0:65]).then_inc(s.rows_t, 1)
        pe.wait_ge(s.xn_ready, 3)
        for k in range(KB):
            if k >= 4:
                pe.wait_ge(s.h_full, k - 3)
            c = slice(P * k, P * k + P)
            pe.transpose(ps[:, k % 4, 0:META], xt[0:META, 0, c], ident[0:META, 0:META])
            pe.transpose(ps[:, k % 4, META:META + P], xt[:, 1, c], ident[:])
            pe.transpose(ps[:, k % 4, META + P:S], xt[:, 2, c], ident[:]).then_inc(s.ht_t, 1)
        pe.wait_ge(s.h_lo, KB)

        def stream(section, hi, lo, c0, before_sem):
            n = S - c0 if section in (XM, OG, KA, QA, VA, GA, GB) else T
            if before_sem is not None:
                pe.wait_ge(*before_sem)
            pe.sem_inc(evac[section], 2)
            with pe.Fori(0, KB // 2) as i:
                for j in range(2):
                    o = ps[:, bank(section, j), 0:n]
                    pe.wait_ge(evac[section], i * 2 + (j + 1))
                    for kh in range(2):
                        b = 2 * j + kh
                        pe.wait_ge(s.lo_ready, i * 4 + (PIECES * section + 2 * j + kh + 1))
                        for kk in range(4):
                            k = 4 * kh + kk
                            w1, w2 = whi[:, b, P * kk:P * kk + P], wlo[:, b, P * kk:P * kk + P]
                            mm(o, w1, hi[:, k, c0:c0 + n], start=(k == 0), stop=False)
                            mm(o, w1, lo[:, k, c0:c0 + n], start=False, stop=False)
                            last = mm(o, w2, hi[:, k, c0:c0 + n], start=False, stop=(k == KB - 1))
                        last.then_inc(s.pieces_used, 1)

        stream(XM, hi_h, lo_h, 0, None)
        stream(OG, hi_h, lo_h, META, None)
        pe.wait_ge(s.wif_split, 3)
        pe.wait_ge(evac[XM], KB + 2)
        o = ps[0:64, 0, 0:S]
        for k in range(KB):
            for n, (w, m) in enumerate(((wif_hi, hi_h), (wif_hi, lo_h), (wif_lo, hi_h))):
                last = mm(o, w[:, k, :], m[:, k, :], start=(k == 0 and n == 0), stop=(k == KB - 1 and n == 2))
        last.then_inc(s.if_done, 1)

        hw = raw[:, slot_of("heads"), :, :].rearrange("p a (b e) -> p (a b) e", e=MD)
        pe.wait_ge(s.heads_in, 48)
        pe.wait_ge(s.xc_ready, KB + 2)
        for g in range(28):
            if g >= 4:
                pe.wait_ge(s.hp_act, g - 3)
            for c in range(2):
                if g < 16:
                    h, eb = divmod(g // 2, 2)
                    w = hw[:, 8 * (g % 2) + 2 * h + c, P * eb:P * eb + P]
                    c0 = META if g % 2 == 0 else 0
                    last = mm(ps[:, 4 + g % 4, 0:S - c0], w, xc[:, 2 * h + c, c0:S], start=(c == 0), stop=(c == 1))
                else:
                    h, st = divmod(g - 16, 3)
                    s0, n = STILES[st]
                    last = mm(ps[0:n, 4 + g % 4, 0:MD], xm[:, 2 * h + c, CONV - 1 + s0:CONV - 1 + s0 + n],
                              hw[:, 16 + 2 * h + c, :], start=(c == 0), stop=(c == 1))
            last.then_inc(s.hp_done, 1)

        pe.wait_ge(s.gates_ready, 1)
        pe.wait_ge(s.hp_act, 28)
        for st, (s0, n) in enumerate(STILES):
            pe.transpose(ps[0:n, 7, MH * st:MH * st + MH], gtmp[:, 0, s0:s0 + n], ident[0:MH, 0:MH])
        for t in range(TT):
            last = pe.transpose(ps[:, 7, 12 + MH * t:12 + MH * t + MH], gtmp[:, 1, META + P * t:META + P * t + P],
                                ident[0:MH, 0:MH])
        last.then_inc(s.gates_t, 1)
        pe.wait_ge(evac[OG], KB + 2)
        for g in range(4):
            t, half = divmod(g, 2)
            for k in range(4):
                last = pe.transpose(ps[:, g, P * k:P * k + P], ot[:, 4 * half + k, P * t:P * t + P], ident[:])
            last.then_inc(s.ot_t, 1)

        def scores(h):
            if h == 0:
                pe.wait_ge(s.aux_ready, 2)
                pe.wait_ge(s.exp_ready, 1)
            if h >= 2:
                pe.wait_ge(s.e_done, h - 1)
            b = 4 + h % 2
            for st, (c0, t0, rows, m0, mn) in enumerate(((0, 0, P, META, 112), (256, 112, P, 0, P),
                                                         (400, 240, META, 0, META))):
                mm(ps[0:rows, b, c0:c0 + T - t0], sel[:, h, 0:rows], mrow[:, META + t0:S], start=True, stop=False,
                   skip_group_check=True)
                last = mm(ps[0:rows, b, c0:c0 + mn], ident[0:rows, 0:rows], late[0:rows, m0:m0 + mn], start=False,
                          stop=True, skip_group_check=True)
            last.then_inc(s.mb_done, 1)
            if h >= 2:
                pe.wait_ge(s.w_done, h - 1)
            b = 6 + h % 2
            for st, (c0, t0, rows) in enumerate(((0, 0, P), (256, 112, P), (400, 240, META))):
                for c in range(2):
                    last = mm(ps[0:rows, b, c0:c0 + T - t0], km[:, 2 * h + c, STILES[st][0]:STILES[st][0] + rows],
                              qm[:, 2 * h + c, t0:T], start=(c == 0), stop=(c == 1))
            last.then_inc(s.sc_done, 1)

        def numerators(h):
            pe.wait_ge(s.w_done, h + 1)
            if h == 0:
                pe.wait_ge(s.ot_ready, 4)
            if h >= 2:
                pe.wait_ge(s.hh_done, TT * (h - 1))
            for t in range(TT):
                tiles = range(2 + t)
                for st in tiles:
                    n = STILES[st][1]
                    last = mm(ps[:, 2 * (h % 2) + t, 0:MD + 1], wgt[0:n, h % 2, st, P * t:P * t + P],
                              vm[0:n, st, h, :], start=(st == 0), stop=(st == tiles[-1]))
            last.then_inc(s.num_done, 1)

        scores(0)
        for h in range(MH):
            if h + 1 < MH:
                scores(h + 1)
            numerators(h)
        pe.wait_ge(s.hh_done, TT * MH)

        stream(KA, hi_h, lo_h, 0, None)
        stream(QA, hi_h, lo_h, META, None)
        stream(VA, hi_h, lo_h, 0, (evac[KA], KB + 2))
        pe.wait_ge(evac[QA], KB + 2)
        pe.wait_ge(evac[VA], KB + 2)
        for g in range(6):
            st, half = divmod(g, 2)
            s0, n = STILES[st]
            if g >= 4:
                pe.wait_ge(s.va_ready, g - 3)
            for k in range(4):
                last = pe.transpose(ps[0:n, 4 + g % 4, P * k:P * k + P], vat[:, 4 * half + k, s0:s0 + n], ident[:])
            last.then_inc(s.va_t, 1)

        def attend(h):
            if h == 0:
                pe.wait_ge(s.va_ready, 6)
            if h >= 2:
                pe.wait_ge(s.exp_done, h - 1)
            for half in range(2):
                b = 4 + 2 * (h % 2) + half
                for t, (c0, n) in enumerate(((0, 144), (144, S))):
                    mm(ps[:, b, c0:c0 + n], qa[:, half, h, P * t:P * t + P], ka[:, h, 0:n], start=True, stop=False,
                       skip_group_check=True)
                    last = mm(ps[:, b, c0 + n - P:c0 + n], ident[:], ahead[:], start=False, stop=True,
                              skip_group_check=True)
            last.then_inc(s.s_done, 1)

        attend(0)
        for h in range(AH):
            if h + 1 < AH:
                attend(h + 1)
            e = h % 2
            pe.wait_ge(s.attn_done, h + 1)
            if h >= 1:
                pe.wait_ge(s.at_act, h)
                pe.wait_ge(s.at_dve, h)
            pe.transpose(ps[:, 0, 0:P], ea[:, e, 0, 0:P], ident[:])
            pe.transpose(ps[:, 0, P:2 * P], ea[:, e, 0, 144:144 + P], ident[:])
            pe.transpose(ps[:, 0, 2 * P:3 * P], ea[:, e, 0, 144 + P:144 + 2 * P], ident[:])
            pe.transpose(ps[0:META, 1, 0:P], ea[:, e, 0, P:P + META], ident[:])
            pe.transpose(ps[0:META, 1, P:2 * P], ea[:, e, 0, 144 + 2 * P:144 + S], ident[:]).then_inc(s.tr_done, 1)
            pe.wait_ge(s.at_act, h + 1)
            pe.wait_ge(s.at_dve, h + 1)
            if h >= 2:
                pe.wait_ge(s.o_copied, h - 1)
            c = slice(P * h, P * h + P)
            b = 2 + h % 2
            mm(ps[:, b, 0:P], att[:, 0:P], va[:, 0, c], start=True, stop=False, skip_group_check=True)
            mm(ps[:, b, 0:P], att2[:, 0:P], va[0:META, 1, c], start=False, stop=True, skip_group_check=True)
            mm(ps[:, b, P:2 * P], att[:, P:2 * P], va[:, 0, c], start=True, stop=False, skip_group_check=True)
            mm(ps[:, b, P:2 * P], att[:, 2 * P:3 * P], va[:, 1, c], start=False, stop=False, skip_group_check=True)
            mm(ps[:, b, P:2 * P], att2[:, P:2 * P], va[0:META, 2, c], start=False, stop=True,
               skip_group_check=True).then_inc(s.av_done, 1)
        stream(GA, hi_h, lo_h, META, (s.o_copied, AH))

        def turn(src, taken, sem_t, ready):
            pe.wait_ge(*ready)
            for j in range(4):
                if taken is not None:
                    pe.wait_ge(taken, 2 * j + 2)
                for k in (2 * j, 2 * j + 1):
                    for t in range(TT):
                        c = T * (k % 2) + P * t
                        last = pe.transpose(ps[:, 4 + j, c:c + P], src[:, t, P * k:P * k + P], ident[:])
                last.then_inc(sem_t, 1)

        turn(hh, None, s.ym_t, (s.hn_ready, TT * MH))
        turn(oall, s.ym_full, s.ya_t, (s.ya_ready, 1))
        pe.wait_ge(s.ya_lo_s, KB)
        stream(WM, ym_hi, ym_lo, 0, (evac[GA], KB + 2))
        stream(GB, hi_h, lo_h, META, None)
        stream(WA, ya_hi, ya_lo, 0, (evac[WM], KB + 2))
        pe.wait_ge(s.mg_lo_s, 2)
        for n in range(PIECES):
            k, half = divmod(n, 2)
            pe.wait_ge(s.lo_ready, OUT_BASE + n + 1)
            for t in range(TT):
                o = ps[:, 4 + 2 * t + half, :]
                c = slice(P * t, P * t + P)
                mm(o, mg_hi[:, k, c], whi[:, n % NBUF, :], start=(k == 0), stop=False)
                mm(o, mg_lo[:, k, c], whi[:, n % NBUF, :], start=False, stop=False)
                last = mm(o, mg_hi[:, k, c], wlo[:, n % NBUF, :], start=False, stop=(k == KB - 1))
            last.then_inc(s.pieces_used, 1)

        pe.wait_ge(evac[GB], KB + 2)
        pe.wait_ge(evac[WA], KB + 2)
        for t in range(TT):
            pe.wait_ge(s.h1_ready, t + 1)
            for half in range(2):
                for k in range(4):
                    c = P * (4 * half + k)
                    last = pe.transpose(ps[:, 2 * t + half, P * k:P * k + P], h1[:, t, c:c + P], ident[:])
                last.then_inc(s.h1_t, 1)
        pe.wait_ge(s.wr_in, 16)
        pe.wait_ge(s.h1t_act, 2)
        pe.wait_ge(s.h1t_dve, 2)
        for k in range(KB):
            last = mm(ps[0:NE, 4, 0:T], wr[:, k, :], h1t[:, k, :], start=(k == 0), stop=(k == KB - 1))
        last.then_inc(s.logit_done, 1)
        pe.wait_ge(s.logit_sb, 1)
        for t in range(TT):
            last = pe.transpose(ps[:, 5, NE * t:NE * t + NE], lgt[:, P * t:P * t + P], ident[0:NE, 0:NE])
        last.then_inc(s.logit_t, 1)
        pe.wait_ge(s.mask_ready, 1)
        g = dict(skip_group_check=True)
        mm(ps[:, 6, 0:NE], before[:], mask[:, 0, :], start=True, stop=True, **g)
        mm(ps[:, 6, NE:2 * NE], ones[:], mask[:, 0, :], start=True, stop=False, **g)
        mm(ps[:, 6, NE:2 * NE], before[:], mask[:, 1, :], start=False, stop=True, **g)
        mm(ps[:, 6, 2 * NE:3 * NE], ones[:], mask[:, 0, :], start=True, stop=False, **g)
        mm(ps[:, 6, 2 * NE:3 * NE], ones[:], mask[:, 1, :], start=False, stop=True, **g).then_inc(s.rank_done, 1)

        pe.wait_ge(s.units_ready, 1)
        pe.sem_inc(s.acc_added, 4)

        def scatter():
            for j in range(4):
                t, c = divmod(j, 2)
                mm(ps[:, 2 + j, :], wpt[:, t, :], zsb[:, 512 * c:512 * c + 512], start=True,
                   stop=True).then_inc(s.scat_done, 1)

        with pe.Fori(0, NE) as e:
            nb = pe.value_load(units[0:1, 0, bass.ds(e, 1)], min_val=1, max_val=MAXBLK)
            first = pe.value_load(units[0:1, 1, bass.ds(e, 1)], min_val=0, max_val=NE * MAXBLK)
            with pe.Fori(0, nb) as b:
                u = pe.snap(first + b)

                def product(j, lhs, bank0, used):
                    for q in range(4):
                        pe.wait_ge(raw_in[ESLOT[j]][q], e * 16 + 16 * (LAP[j] + 1))
                        for c in range(2):
                            for k in (2 * q, 2 * q + 1):
                                r0 = SLOTS * (k % 2)
                                last = mm(ps[r0:r0 + SLOTS, bank0 + c, :], lhs[:, k, :],
                                          raw[:, ESLOT[j], k, 512 * c:512 * c + 512], start=(q == 0), stop=(q == 3))
                        last.then_inc(used, 1)

                pe.wait_ge(s.pick_ready, u * 2 + 2)
                pe.wait_ge(s.acc_added, u * 4 + 4)
                pe.wait_ge(s.wpt_ready, u + 1)
                for k in range(KB):
                    for t in range(TT):
                        last = mm(ps[:, 4 + k // 4, P * (k % 4):P * (k % 4) + P], h1[:, t, P * k:P * k + P],
                                  pick[:, t, :], start=(t == 0), stop=(t == 1))
                last.then_inc(s.gath_done, 1)
                pe.wait_ge(s.xg_ready, u + 1)
                product(0, xg, 0, s.gate_used)
                product(1, xg, 2, s.up_used)
                pe.wait_ge(s.gsb_ready, u * 2 + 2)
                for k in range(KB):
                    last = pe.transpose(ps[:, 4 + k // 4, P * (k % 4):P * (k % 4) + P], gsb[:, P * k:P * k + P], ident[:])
                last.then_inc(s.tg_done, 1)
                pe.wait_ge(s.usb_ready, u * 2 + 2)
                for k in range(KB):
                    last = pe.transpose(ps[:, k // 4, P * (k % 4):P * (k % 4) + P], usb[:, P * k:P * k + P], ident[:])
                last.then_inc(s.tu_done, 1)
                pe.wait_ge(s.gate_ready, u + 1)
                pe.wait_ge(s.z_ready, u * 2 + 2)
                scatter()
                pe.wait_ge(s.hid_ready, u + 1)
                product(2, hid, 6, s.down_used)
                pe.wait_ge(s.wpick_ready, u * 2 + 2)
                for t in range(TT):
                    last = pe.transpose(ps[:, 0, P * t:P * t + P], wpick[:, t, :], ident[:])
                last.then_inc(s.wpt_t, 1)
        end = pe.value_load(units[0:1, 2, NE - 1:NE], min_val=0, max_val=NE * MAXBLK)
        pe.wait_ge(s.acc_added, end * 4 + 8)
        pe.wait_ge(s.wpt_ready, end + 2)
        pe.wait_ge(s.z_ready, end * 2 + 4)
        scatter()




_INS = ['x', 'meta_tokens', 'ln_in_g', 'ln_in_b', 'w_in', 'conv_w', 'conv_b', 'wq_m', 'wk_m', 'wv_m', 'b_i', 'b_f',
        'm_norm_g', 'lam_q1', 'lam_k1', 'lam_q2', 'lam_k2', 'a_norm_g', 'w_branch_m', 'w_branch_a', 'w_out',
        'ln1_g', 'ln1_b', 'ln2_g', 'ln2_b', 'w_router', 'router_bias', 'w_gate_e', 'w_up_e', 'w_down_e']
_OUTS = [((1, T, D), 'float32')]


def kernel(**inputs):
    import numpy as _np
    import concourse.bacc as _bacc
    from concourse.bass_utils import run_bass_kernel_spmd as _run

    nc = _bacc.Bacc("TRN2", target_bir_lowering=False, num_devices=1)
    arrays, args = {}, []
    for name in _INS:
        a = _np.ascontiguousarray(inputs[name])
        arrays[f"in_{name}_dram"] = a
        args.append(nc.dram_tensor(f"in_{name}_dram", a.shape, mybir.dt.from_np(a.dtype), kind="ExternalInput").ap())
    for i, (shape, dtype) in enumerate(_OUTS):
        dt = mybir.dt.from_np(_np.dtype(dtype))
        args.append(nc.dram_tensor(f"out_{i}_dram", shape, dt, kind="ExternalOutput").ap())
    with ExitStack() as ctx:
        build(ctx, nc, *args)
    r = _run(nc, [arrays], core_ids=[0])
    return r.results[0]["out_0_dram"]
```

```python
import math
from contextlib import ExitStack


import concourse.bass as bass
from concourse import mybir

F32 = mybir.dt.float32
F32R = mybir.dt.float32r
I32 = mybir.dt.int32
BF16 = mybir.dt.bfloat16
ALU = mybir.AluOpType
ACT = mybir.ActivationFunctionType
AX = mybir.AxisListType

P = 128
D = 1024
KB = D // P
META = 16
T = 256
S = META + T
TT = T // P
STILES = ((0, P), (P, P), (2 * P, META))
MH, MD = 4, 256
AH, AD, AV = 8, 64, 128
CONV = 4
NE, NG, EPG = 16, 4, 4
SLOTS = 64
MAXBLK = T // SLOTS
UNITS = NE + 2 * T // SLOTS + 2
D_IN = 7176
ALPHA = 2.0 ** 0.25
LAM_INIT = 0.8 - 0.6 * math.exp(-0.3 * 0)
EPS = 1e-5
BIG = 1e30

XM, OG, KA, QA, VA, GA, WM, GB, WA = range(9)
COLUMN = {XM: 0, OG: 1024, QA: 2056, KA: 3080, VA: 4104, GA: 5128, GB: 6152}
MATRICES = [XM, OG, "heads", KA, QA, VA, GA, WM, GB, WA, "out"]
PIECES = 2 * KB
NBUF = 4
OUT_BASE = PIECES * 9
FIRST_E = len(MATRICES)
LAP = [(FIRST_E + j) // 3 - ((FIRST_E + j) % 3 == MATRICES.index("heads") % 3) for j in range(3)]
ESLOT = [(FIRST_E + j) % 3 for j in range(3)]


def slot_of(section):
    return MATRICES.index(section) % 3


def lap_of(section):
    m, heads = MATRICES.index(section), MATRICES.index("heads")
    return m // 3 + 1 - (m > heads and m % 3 == heads % 3)


class Semaphores:
    pass


class Steps:

    def __init__(self, eng, sem):
        self.eng, self.sem, self.n, self.base = eng, sem, 0, 0

    def __call__(self, ins):
        self.n += 1
        return ins.then_inc(self.sem, 1)

    def settle(self):
        self.eng.wait_ge(self.sem, self.base + self.n)


def build(ctx, nc, x, meta, ln_in_g, ln_in_b, w_in, conv_w, conv_b, wq, wk, wv, b_i, b_f, m_norm_g,
          lam_q1, lam_k1, lam_q2, lam_k2, a_norm_g, w_bm, w_ba, w_out, ln1_g, ln1_b, ln2_g, ln2_b,
          w_router, router_bias, w_gate, w_up, w_down, out):
    top = [(nc.sbuf_base + 63) // 64 * 64]

    def bytes_of(shape, dt):
        n = 2 if dt == BF16 else 4
        for d in shape[1:]:
            n *= d
        return n

    def perm(name, shape, dt=F32):
        t = nc.alloc_sbuf_tensor_at(name, shape, dt, offset=top[0])
        top[0] += (bytes_of(shape, dt) + 31) // 32 * 32
        return t

    raw = perm("raw", [P, 3, KB, D])
    split_area = top[0]
    whi = perm("whi", [P, NBUF, 4 * P], F32R)
    wlo = perm("wlo", [P, NBUF, 4 * P], F32R)
    ident = perm("ident", [P, P])
    ident_b = perm("ident_b", [P, P], BF16)
    late_b = perm("late_b", [P, P], BF16)
    ahead_b = perm("ahead_b", [P, P], BF16)
    before = perm("before", [P, P])
    ones = perm("ones", [P, P])
    slotno = perm("slotno", [P, 2, SLOTS])
    sel = perm("sel", [MH, MH, P])
    boff = perm("boff", [P, MAXBLK])
    minus_half = perm("minus_half", [P, 2 * AH])
    rank16 = perm("rank16", [P, NE])
    unitno = perm("unitno", [1, UNITS])
    chan = perm("chan", [P, 81])
    mrow = perm("mrow", [MH, S])
    at_col = perm("at_col", [P, 3, MH])
    em_col = perm("em_col", [P, TT, MH])
    gate_bias = perm("gate_bias", [MH, 2])
    wr = perm("wr", [P, KB, NE])
    rbias = perm("rbias", [P, NE])
    stats = perm("stats", [P, 3, 2, 6])
    mv = perm("mv", [P, 3, 2])
    ve = perm("ve", [P, 3])
    rstd = perm("rstd", [P, 3])
    stats8 = perm("stats8", [P, TT * MH, 6])
    mv8 = perm("mv8", [P, TT * MH, 2])
    ve8 = perm("ve8", [P, TT * MH])
    rstd8 = perm("rstd8", [P, TT * MH])
    den = perm("den", [P, MH, TT])
    rden = perm("rden", [P, MH, TT])
    neglam = perm("neglam", [P, 1])
    nmax = perm("nmax", [P, 2, TT, 2])
    rsum = perm("rsum", [P, 2, TT, 2])
    rinv = perm("rinv", [P, 2, TT, 2])
    ssq = perm("ssq", [P, TT * AH])
    vea = perm("vea", [P, TT * AH])
    rstda = perm("rstda", [P, TT * AH])
    work = (top[0] + 63) // 64 * 64

    def at(name, shape, offset, dt=F32):
        return nc.alloc_sbuf_tensor_at(name, shape, dt, offset=work + offset)

    hi_h = at("hi_h", [P, KB, S], 0, F32R)
    lo_h = at("lo_h", [P, KB, S], 8704, F32R)
    hres = at("hres", [P, TT, D], 17408)
    F = 25600
    xt = at("xt", [P, 3, D], F)
    rows_in = at("rows_in", [P, 2, D], F + 12288)
    hfull = at("hfull", [P, 2, S], F + 20480)
    crow = at("crow", [81, P], F + 22656)
    lamv = at("lamv", [P, 4, AD], F + 23168)
    lamp = at("lamp", [P, 2, AD], F + 24192)
    lams = at("lams", [P, 4], F + 24704)
    wif = at("wif", [P, KB, 2 * MH], F + 24736)
    wif_hi = at("wif_hi", [P, KB, 64], F + 24992, F32R)
    wif_lo = at("wif_lo", [P, KB, 64], F + 27040, F32R)
    qm = at("qm", [P, KB, T], F)
    km = at("km", [P, KB, S], F + 8192)
    vm = at("vm", [P, 3, MH, MD + 1], F + 16896)
    xm = at("xm", [P, KB, S + CONV - 1], F + 29248)
    xc = at("xc", [P, KB, S], F + 38048)
    ot = at("ot", [P, KB, T], F + 46752)
    late = at("late", [P, P], F + 38048)
    ahead = at("ahead", [P, P], F + 38560)
    SCAN = 2 * P
    scan = at("scan", [MH, 3, SCAN + S], F + 55296)
    gtmp = at("gtmp", [MH, 2, S], F + 61632)
    wgt = at("wgt", [P, 2, 3, T], F + 29248)
    ex = at("ex", [P, 2, 416], F + 35392)
    csig = at("csig", [P, 2, S], F + 16896)
    hh = at("hh", [P, TT, D], F + 55616)
    va = at("va", [P, 3, D], F)
    qa = at("qa", [P, 2, KB, T], F + 12288)
    vat = at("vat", [P, KB, S], F + 28672)
    oall = at("oall", [P, TT, D], F + 28672)
    att2 = at("att2", [META, 2 * P], F + 37376)
    ka = at("ka", [P, KB, S], F + 38720)
    ea = at("ea", [P, 2, 2, 416], F + 47424)
    att = at("att", [P, 3 * P], F + 54080)
    junk = at("junk", [P, P], F + 36864)
    ym_hi = at("ym_hi", [P, KB, T], F, F32R)
    ym_lo = at("ym_lo", [P, KB, T], F + 8192, F32R)
    ya_hi = at("ya_hi", [P, KB, T], F + 36864, F32R)
    ya_lo = at("ya_lo", [P, KB, T], F + 45056, F32R)
    sg = at("sg", [P, KB, T], F + 16384)
    merged = at("merged", [P, KB, T], F + 24576)
    mtmp = at("mtmp", [P, 2, T], F + 53248)
    mg_hi = at("mg_hi", [P, KB, T], 0, F32R)
    mg_lo = at("mg_lo", [P, KB, T], 8192, F32R)
    h1 = at("h1", [P, TT, D], F)
    acc = at("acc", [P, TT, D], F + 8192)
    h1t = at("h1t", [P, KB, T], 0)
    lgt = at("lgt", [NE, T], F + 16384)
    rt = at("rt", [P, 16, TT * NE], F + 17408)
    gsb = at("gsb", [P, D], 9216)
    usb = at("usb", [P, D], 13312)
    gate = at("gate", [P, KB, SLOTS], split_area - work)
    gsig = at("gsig", [P, KB, SLOTS], split_area + 2048 - work)
    upv = at("upv", [P, KB, SLOTS], split_area + 4096 - work)
    hid = at("hid", [P, KB, SLOTS], split_area + 6144 - work)
    mask = at("mask", [P, TT, NE], F + 19456)
    comb = at("comb", [P, TT, NE], F + 19584)
    slot = at("slot", [P, TT, NE], F + 19712)
    counts = at("counts", [1, NE], F + 19840)
    nblk_f = at("nblk_f", [1, NE], F + 19904)
    ends_f = at("ends_f", [1, 2, 32 + NE], F + 19968)
    blocks = at("blocks", [1, 3, NE], F + 20352, I32)
    unit_of = at("unit_of", [1, 2, UNITS], F + 20544, I32)
    total = at("total", [1, 1], F + 20768, I32)
    table_load = at("table_load", [1, 1], F + 20800)
    unit_f = at("unit_f", [1, 2, UNITS], F + 20832)
    passed = at("passed", [1, UNITS, NE], F + 21056)
    gate_x = at("gate_x", [P, KB, D], F + 31264)
    up_x = (at("up_x0", [P, 2, D], split_area + 8192 - work),
            at("up_x1", [P, 2, D], 0))
    zsb = at("zsb", [P, D], 17408)
    xg = at("xg", [P, KB, SLOTS], 17408 + 4096)
    pick = at("pick", [P, TT, 2 * SLOTS], 17408 + 6144)
    wpick = at("wpick", [P, TT, 2 * SLOTS], 17408 + 7168)
    wpt = at("wpt", [P, TT, P], 8192)
    rows1 = at("rows1", [P, 2, D], F + 23072)

    ps = nc.alloc_psum_tensor("ps", [P, 8, 512], F32)
    turned1 = ps[:, 0:4, :].rearrange("p a (b c) -> p (a b) c", c=T)

    s = Semaphores()
    s.x_in0 = nc.alloc_semaphore("x_in0")
    s.x_in1 = nc.alloc_semaphore("x_in1")
    s.x_in2 = nc.alloc_semaphore("x_in2")
    s.crow_in = nc.alloc_semaphore("crow_in")
    s.rows_in_in = nc.alloc_semaphore("rows_in_in")
    s.gb_in = nc.alloc_semaphore("gb_in")
    s.lam_in = nc.alloc_semaphore("lam_in")
    s.wif_in = nc.alloc_semaphore("wif_in")
    s.wr_in = nc.alloc_semaphore("wr_in")
    s.rb_in = nc.alloc_semaphore("rb_in")
    s.heads_in = nc.alloc_semaphore("heads_in")
    s.rows1_in = nc.alloc_semaphore("rows1_in")
    s.rows2_in = nc.alloc_semaphore("rows2_in")
    s.stored = nc.alloc_semaphore("stored")
    s.masks_ready = nc.alloc_semaphore("masks_ready")
    s.consts = nc.alloc_semaphore("consts")
    s.dve = nc.alloc_semaphore("dve")
    s.act = nc.alloc_semaphore("act")
    s.pool = nc.alloc_semaphore("pool")
    s.xn_ready = nc.alloc_semaphore("xn_ready")
    s.var_ready = nc.alloc_semaphore("var_ready")
    s.rstd_ready = nc.alloc_semaphore("rstd_ready")
    s.hres_ready = nc.alloc_semaphore("hres_ready")
    s.rows_t = nc.alloc_semaphore("rows_t")
    s.chan_ready = nc.alloc_semaphore("chan_ready")
    s.ht_t = nc.alloc_semaphore("ht_t")
    s.h_full = nc.alloc_semaphore("h_full")
    s.h_hi = nc.alloc_semaphore("h_hi")
    s.h_lo = nc.alloc_semaphore("h_lo")
    s.wif_split = nc.alloc_semaphore("wif_split")
    s.if_done = nc.alloc_semaphore("if_done")
    s.hi_ready = nc.alloc_semaphore("hi_ready")
    s.lo_ready = nc.alloc_semaphore("lo_ready")
    s.pieces_used = nc.alloc_semaphore("pieces_used")
    s.conv_acc = nc.alloc_semaphore("conv_acc")
    s.conv_sig = nc.alloc_semaphore("conv_sig")
    s.xc_ready = nc.alloc_semaphore("xc_ready")
    s.hp_done = nc.alloc_semaphore("hp_done")
    s.hp_act = nc.alloc_semaphore("hp_act")
    s.ot_t = nc.alloc_semaphore("ot_t")
    s.ot_ready = nc.alloc_semaphore("ot_ready")
    s.gates_ready = nc.alloc_semaphore("gates_ready")
    s.gates_t = nc.alloc_semaphore("gates_t")
    s.aux_ready = nc.alloc_semaphore("aux_ready")
    s.scan_e = nc.alloc_semaphore("scan_e")
    s.scan_l = nc.alloc_semaphore("scan_l")
    s.exp_ready = nc.alloc_semaphore("exp_ready")
    s.mb_done = nc.alloc_semaphore("mb_done")
    s.sc_done = nc.alloc_semaphore("sc_done")
    s.e_done = nc.alloc_semaphore("e_done")
    s.w_done = nc.alloc_semaphore("w_done")
    s.num_done = nc.alloc_semaphore("num_done")
    s.hh_done = nc.alloc_semaphore("hh_done")
    s.var8 = nc.alloc_semaphore("var8")
    s.rstd8_ready = nc.alloc_semaphore("rstd8_ready")
    s.hn_ready = nc.alloc_semaphore("hn_ready")
    s.vm_ones = nc.alloc_semaphore("vm_ones")
    s.qa_zero = nc.alloc_semaphore("qa_zero")
    s.va_t = nc.alloc_semaphore("va_t")
    s.va_ready = nc.alloc_semaphore("va_ready")
    s.lam_sum = nc.alloc_semaphore("lam_sum")
    s.lam_exp = nc.alloc_semaphore("lam_exp")
    s.s_done = nc.alloc_semaphore("s_done")
    s.nmax_done = nc.alloc_semaphore("nmax_done")
    s.exp_done = nc.alloc_semaphore("exp_done")
    s.attn_done = nc.alloc_semaphore("attn_done")
    s.tr_done = nc.alloc_semaphore("tr_done")
    s.at_act = nc.alloc_semaphore("at_act")
    s.at_dve = nc.alloc_semaphore("at_dve")
    s.av_done = nc.alloc_semaphore("av_done")
    s.o_copied = nc.alloc_semaphore("o_copied")
    s.o_squared = nc.alloc_semaphore("o_squared")
    s.vara = nc.alloc_semaphore("vara")
    s.rstda_ready = nc.alloc_semaphore("rstda_ready")
    s.ya_ready = nc.alloc_semaphore("ya_ready")
    s.ym_t = nc.alloc_semaphore("ym_t")
    s.ym_hi_s = nc.alloc_semaphore("ym_hi_s")
    s.ym_lo_s = nc.alloc_semaphore("ym_lo_s")
    s.ya_t = nc.alloc_semaphore("ya_t")
    s.ya_hi_s = nc.alloc_semaphore("ya_hi_s")
    s.ya_lo_s = nc.alloc_semaphore("ya_lo_s")
    s.ym_full = nc.alloc_semaphore("ym_full")
    s.ya_full = nc.alloc_semaphore("ya_full")
    s.merged_s = nc.alloc_semaphore("merged_s")
    s.mg_hi_s = nc.alloc_semaphore("mg_hi_s")
    s.mg_lo_s = nc.alloc_semaphore("mg_lo_s")
    s.resid_done = nc.alloc_semaphore("resid_done")
    s.var1 = nc.alloc_semaphore("var1")
    s.rstd1 = nc.alloc_semaphore("rstd1")
    s.xn1_ready = nc.alloc_semaphore("xn1_ready")
    s.h1_ready = nc.alloc_semaphore("h1_ready")
    s.acc_ready = nc.alloc_semaphore("acc_ready")
    s.h1_t = nc.alloc_semaphore("h1_t")
    s.h1t_act = nc.alloc_semaphore("h1t_act")
    s.h1t_dve = nc.alloc_semaphore("h1t_dve")
    s.logit_done = nc.alloc_semaphore("logit_done")
    s.logit_sb = nc.alloc_semaphore("logit_sb")
    s.logit_t = nc.alloc_semaphore("logit_t")
    s.router_exp = nc.alloc_semaphore("router_exp")
    s.exp_r = nc.alloc_semaphore("exp_r")
    s.mask_ready = nc.alloc_semaphore("mask_ready")
    s.rank_done = nc.alloc_semaphore("rank_done")
    s.units_ready = nc.alloc_semaphore("units_ready")
    s.pick_ready = nc.alloc_semaphore("pick_ready")
    s.gath_done = nc.alloc_semaphore("gath_done")
    s.xg_ready = nc.alloc_semaphore("xg_ready")
    s.gate_used = nc.alloc_semaphore("gate_used")
    s.up_used = nc.alloc_semaphore("up_used")
    s.down_used = nc.alloc_semaphore("down_used")
    s.gsb_ready = nc.alloc_semaphore("gsb_ready")
    s.tg_done = nc.alloc_semaphore("tg_done")
    s.gate_ready = nc.alloc_semaphore("gate_ready")
    s.gsig_ready = nc.alloc_semaphore("gsig_ready")
    s.usb_ready = nc.alloc_semaphore("usb_ready")
    s.tu_done = nc.alloc_semaphore("tu_done")
    s.hid_ready = nc.alloc_semaphore("hid_ready")
    s.scat_done = nc.alloc_semaphore("scat_done")
    s.acc_added = nc.alloc_semaphore("acc_added")
    s.wpt_t = nc.alloc_semaphore("wpt_t")
    s.wpt_ready = nc.alloc_semaphore("wpt_ready")
    s.z_ready = nc.alloc_semaphore("z_ready")
    s.wpick_ready = nc.alloc_semaphore("wpick_ready")
    s.moe_dve = nc.alloc_semaphore("moe_dve")
    s.fin_var = nc.alloc_semaphore("fin_var")
    s.fin_rstd = nc.alloc_semaphore("fin_rstd")
    s.fin_ready = nc.alloc_semaphore("fin_ready")
    raw_in = [[nc.alloc_semaphore(f"raw_in_{a}_{q}") for q in range(4)] for a in range(3)]
    evac = [nc.alloc_semaphore(f"evac_{n}") for n in range(9)]

    gate_x_in = [nc.alloc_semaphore(f"gate_x_in_{q}") for q in range(4)]
    up_x_in = [nc.alloc_semaphore(f"up_x_in_{q}") for q in range(2)]

    block = ctx.enter_context(nc.Block())

    def raw_quarter(slot_no, q):
        return raw[:, slot_no, 2 * q:2 * q + 2, :]

    def rows_of(w, q):
        return w[256 * q:256 * q + 256, :].rearrange("(j p) c -> p j c", p=P)

    def piece(section, blk, kh):
        a = slot_of(section)
        return raw[:, a, 4 * kh:4 * kh + 4, bass.ds(blk * P, P)]

    def out_piece(n):
        return raw[:, slot_of("out"), n // 2, 512 * (n % 2):512 * (n % 2) + 512]

    def bank(section, blk_odd):
        return 2 * (section % 2) + blk_odd

    def c_conv(w, blk):
        return chan[:, bass.ds(w * KB + blk, 1)]

    C_CONVB, C_LNG, C_LNB, C_MG, C_AG, C_L1G, C_L1B = 32, 40, 48, 56, 64, 65, 73

    @block.sync
    def _(sp):
        dram = {WM: w_bm[0], WA: w_ba[0], "out": w_out[0]}
        free = {KA: ("lo", 1), QA: ("lo", 2), VA: ("heads", 0), GA: ("lo", 3), WM: ("lo", 4),
                GB: ("lo", 5), WA: ("lo", 6), "out": ("lo", 7)}
        for j in range(3):
            src = meta if j == 0 else x[0, P * (j - 1):P * j, :]
            sp.dma_start(xt[0:src.shape[0], j, :], src).then_inc((s.x_in0, s.x_in1, s.x_in2)[j], 16)
        sp.wait_ge(s.x_in1, 16)
        for m, what in enumerate(MATRICES):
            if what == OG:
                sp.wait_ge(raw_in[0][0], 16)
                for j, v in enumerate((ln_in_g, ln_in_b)):
                    sp.dma_start(rows_in[:, j, :], v.partition_broadcast(P)).then_inc(s.rows_in_in, 16)
            if what == KA:
                sp.dma_start(wr[:], w_router.rearrange("(k p) e -> p k e", p=P)).then_inc(s.wr_in, 16)
                sp.dma_start(rbias[:], router_bias.partition_broadcast(P)).then_inc(s.rb_in, 16)
            if what == "heads":
                for j, w in enumerate((wq, wk, wv)):
                    sp.dma_start(raw[:, m % 3, 2 * j:2 * j + 2, :].rearrange("p a (b e) -> p (a b) e", e=MD),
                                 w[0].rearrange("h (c p) e -> p (h c) e", p=P)).then_inc(s.heads_in, 16)
                continue
            if what in free:
                kind, done = free[what]
                if kind == "lo":
                    sp.wait_ge(s.lo_ready, PIECES * done)
                else:
                    sp.wait_ge(s.hp_done, 28)
            for q in range(4):
                if what == XM:
                    sp.dma_start(raw[:, 0, :, 256 * q:256 * q + 256],
                                 w_in[0, :, 256 * q:256 * q + 256].rearrange("(k p) c -> p k c", p=P)
                                 ).then_inc(raw_in[0][q], 16)
                    continue
                if what in dram:
                    src = rows_of(dram[what], q)
                else:
                    src = rows_of(w_in[0, :, COLUMN[what]:COLUMN[what] + D], q)
                sp.dma_start(raw_quarter(m % 3, q), src).then_inc(raw_in[m % 3][q], 16)

        for j, (w, done) in enumerate(((w_gate, 8), (w_up, 9), (w_down, 10))):
            if j == 2:
                sp.wait_ge(s.mg_lo_s, KB)
                for q in range(4):
                    sp.dma_start(gate_x[:, 2 * q:2 * q + 2, :], rows_of(w_gate[0, 1], q)).then_inc(gate_x_in[q], 16)
            sp.wait_ge(s.lo_ready, PIECES * done)
            for q in range(4):
                sp.dma_start(raw_quarter(ESLOT[j], q), rows_of(w[0, 0], q)).then_inc(raw_in[ESLOT[j]][q], 16)
        for q, (read, n) in enumerate(((s.pieces_used, OUT_BASE + PIECES + NBUF), (s.logit_done, 1))):
            sp.wait_ge(read, n)
            sp.dma_start(up_x[q][:], rows_of(w_up[0, 1], q)).then_inc(up_x_in[q], 16)
        sp.wait_ge(s.units_ready, 1)

        def expert_rows(w, e, q):
            return w[0, bass.ds(e, 1), 256 * q:256 * q + 256, :].rearrange("e (j p) c -> p (e j) c", p=P)

        def last_block(e):
            return sp.value_load(blocks[0:1, 2, bass.ds(e, 1)], min_val=0, max_val=UNITS)

        def fetch_gate(e, odd):
            last = last_block(e - 2)
            for q in range(4):
                sp.wait_ge(s.gate_used, last * 4 + (q + 1))
                if odd:
                    sp.dma_start(gate_x[:, 2 * q:2 * q + 2, :], expert_rows(w_gate, e, q)).then_inc(gate_x_in[q], 16)
                else:
                    sp.dma_start(raw_quarter(ESLOT[0], q), expert_rows(w_gate, e, q)).then_inc(raw_in[ESLOT[0]][q], 16)

        def fetch_rest(e, odd):
            first = isinstance(e, int) and e == 1
            if not first:
                last = last_block(e - 2)
                for q in range(2):
                    sp.wait_ge(s.up_used, last * 4 + (q + 1))
                    if odd:
                        sp.dma_start(up_x[q][:], expert_rows(w_up, e, q)).then_inc(up_x_in[q], 16)
                    else:
                        sp.dma_start(raw_quarter(ESLOT[1], q), expert_rows(w_up, e, q)).then_inc(raw_in[ESLOT[1]][q], 16)
            last = last_block(e - 1)
            for q in (2, 3):
                sp.wait_ge(s.up_used, last * 4 + (q + 1))
                sp.dma_start(raw_quarter(ESLOT[1], q), expert_rows(w_up, e, q)).then_inc(raw_in[ESLOT[1]][q], 16)
            for q in range(4):
                sp.wait_ge(s.down_used, last * 4 + (q + 1))
                sp.dma_start(raw_quarter(ESLOT[2], q), expert_rows(w_down, e, q)).then_inc(raw_in[ESLOT[2]][q], 16)

        fetch_gate(2, False)
        fetch_rest(1, True)
        half = NE // 4 - 1
        with sp.Fori(0, half) as i:
            fetch_gate(i * 2 + 3, True)
            fetch_rest(i * 2 + 2, False)
            fetch_gate(i * 2 + 4, False)
            fetch_rest(i * 2 + 3, True)
        with sp.Fori(half, NE // 2 - 2) as i:
            fetch_rest(i * 2 + 2, False)
            fetch_gate(i * 2 + 3, True)
            fetch_rest(i * 2 + 3, True)
            fetch_gate(i * 2 + 4, False)
        fetch_rest(NE - 2, False)
        fetch_gate(NE - 1, True)
        fetch_rest(NE - 1, True)
        for t in range(TT):
            sp.wait_ge(s.fin_ready, t + 1)
            sp.dma_start(out[0, P * t:P * t + P, :], acc[:, t, :]).then_inc(s.stored, 16)
        sp.wait_ge(s.stored, 16 * TT)

    @block.gpsimd
    def _(pool):
        own = Steps(pool, s.pool)
        for t, v in ((ident, 0.0), (late, 0.0), (ahead, 0.0), (before, 1.0), (sel, 0.0), (ones, 1.0),
                     (minus_half, -0.5)):
            own(pool.memset(t[:], v))
        own(pool.memset(wif_hi[:].bitcast(F32), 0.0))
        own(pool.memset(wif_lo[:].bitcast(F32), 0.0))
        own(pool.memset(xm[:, :, 0:CONV - 1], 0.0))
        own(pool.iota(slotno[:], pattern=[[0, 2], [1, SLOTS]], base=0, channel_multiplier=0,
                      allow_small_or_imprecise_dtypes=True))
        own(pool.iota(boff[:], pattern=[[SLOTS, MAXBLK]], base=0, channel_multiplier=0,
                      allow_small_or_imprecise_dtypes=True))
        own(pool.iota(unitno[:], pattern=[[1, UNITS]], base=0, channel_multiplier=0,
                      allow_small_or_imprecise_dtypes=True))
        own(pool.iota(rank16[:], pattern=[[-1, NE]], base=NE, channel_multiplier=0,
                      allow_small_or_imprecise_dtypes=True))
        own.settle()
        own(pool.affine_select(out=ident[:], in_=ident[:], compare_op=ALU.not_equal, fill=1.0, base=0,
                               pattern=[[-1, P]], channel_multiplier=1))
        own(pool.affine_select(out=late[:], in_=late[:], compare_op=ALU.is_gt, fill=BIG, base=1,
                               pattern=[[1, P]], channel_multiplier=-1))
        own(pool.affine_select(out=ahead[:], in_=ahead[:], compare_op=ALU.is_gt, fill=-BIG, base=1,
                               pattern=[[-1, P]], channel_multiplier=1))
        own(pool.affine_select(out=before[:], in_=before[:], compare_op=ALU.is_gt, fill=0.0, base=0,
                               pattern=[[1, P]], channel_multiplier=-1))
        own(pool.affine_select(out=sel[:], in_=sel[:], compare_op=ALU.not_equal, fill=1.0, base=0,
                               pattern=[[-1, MH], [0, P]], channel_multiplier=1))
        own.settle()
        pool.drain().then_inc(s.consts, 1)
        pool.wait_ge(s.var_ready, 3)
        pool.tensor_tensor(rstd[0:META, 0:1], ve[0:META, 0:1], minus_half[0:META, 0:1],
                           ALU.pow).then_inc(s.rstd_ready, 1)
        pool.tensor_tensor(rstd[:, 1:3], ve[:, 1:3], minus_half[:, 1:3], ALU.pow).then_inc(s.rstd_ready, 1)
        pool.wait_ge(s.xn_ready, 3)
        pool.wait_ge(s.rows_in_in, 32)
        own(pool.tensor_tensor(hres[:], xt[:, 1:3, :], rows_in[:, 0, :].unsqueeze(1).to_broadcast([P, TT, D]),
                               ALU.mult))
        own.settle()
        pool.tensor_tensor(hres[:], hres[:], rows_in[:, 1, :].unsqueeze(1).to_broadcast([P, TT, D]),
                           ALU.add).then_inc(s.hres_ready, 1)
        pool.sem_inc(s.xc_ready, 2)
        with pool.Fori(0, KB // 2) as i:
            for j in range(2):
                pool.wait_ge(s.conv_sig, i * 2 + (j + 1))
                pool.tensor_tensor(xc[:, bass.ds(i * 2 + j, 1), :], xc[:, bass.ds(i * 2 + j, 1), :],
                                   csig[:, j:j + 1, :], ALU.mult).then_inc(s.xc_ready, 1)
        pool.wait_ge(s.if_done, 1)
        pool.wait_ge(s.xc_ready, KB + 2)
        pool.memset(vm[:, :, :, MD:MD + 1], 1.0).then_inc(s.vm_ones, 1)
        pool.wait_ge(s.hp_done, 28)
        for b in range(2):
            pool.memset(wgt[:, b, 1, 0:112], 0.0).then_inc(s.vm_ones, 1)
            pool.wait_ge(s.vm_ones, 2 + 2 * b)
            pool.memset(wgt[0:META, b, 2, 0:240], 0.0).then_inc(s.vm_ones, 1)
            pool.wait_ge(s.vm_ones, 3 + 2 * b)
        pool.wait_ge(s.num_done, MH)
        pool.memset(qa[AD:P, 0, :, :], 0.0).then_inc(s.qa_zero, 1)
        pool.wait_ge(s.qa_zero, 1)
        pool.memset(qa[0:AD, 1, :, :], 0.0).then_inc(s.qa_zero, 1)
        pool.wait_ge(s.qa_zero, 2)
        pool.wait_ge(s.var8, 1)
        pool.tensor_tensor(rstd8[:], ve8[:], minus_half[:, 0:TT * MH], ALU.pow).then_inc(s.rstd8_ready, 1)
        pool.wait_ge(s.vara, 1)
        pool.tensor_tensor(rstda[:], vea[:], minus_half[:], ALU.pow).then_inc(s.rstda_ready, 1)
        for t in range(TT):
            pool.wait_ge(s.var1, t + 1)
            pool.tensor_tensor(rstd[:, t:t + 1], ve[:, t:t + 1], minus_half[:, t:t + 1], ALU.pow).then_inc(s.rstd1, 1)
        pool.wait_ge(s.h1_t, 4)
        pool.wait_ge(s.xn1_ready, TT)
        pool.wait_ge(s.rows1_in, 32)
        own(pool.tensor_tensor(h1[:], h1[:], rows1[:, 0, :].unsqueeze(1).to_broadcast([P, TT, D]), ALU.mult))
        own.settle()
        pool.tensor_tensor(h1[:], h1[:], rows1[:, 1, :].unsqueeze(1).to_broadcast([P, TT, D]),
                           ALU.add).then_inc(s.h1_ready, 1)
        pool.wait_ge(s.resid_done, 2 * TT)
        pool.memset(zsb[:], 0.0).then_inc(s.z_ready, 2)
        pool.memset(wpt[:], 0.0).then_inc(s.wpt_ready, 1)
        for t in range(TT):
            pool.wait_ge(s.fin_var, t + 1)
            pool.tensor_tensor(rstd[:, t:t + 1], ve[:, t:t + 1], minus_half[:, t:t + 1], ALU.pow).then_inc(s.fin_rstd, 1)

    @block.scalar
    def _(act):
        for r0, v in ((0, conv_w[0].rearrange("w (b c) -> (w b) c", c=P)), (32, conv_b[0].rearrange("(b c) -> b c", c=P)),
                      (40, ln_in_g.rearrange("(b c) -> b c", c=P)), (48, ln_in_b.rearrange("(b c) -> b c", c=P)),
                      (56, m_norm_g[0].rearrange("(b c) -> b c", c=P)), (64, a_norm_g),
                      (65, ln1_g[0].rearrange("(b c) -> b c", c=P)), (73, ln1_b[0].rearrange("(b c) -> b c", c=P))):
            act.dma_start(crow[r0:r0 + v.shape[0], :], v).then_inc(s.crow_in, 16)
        with nc.allow_non_contiguous_dma(reason="a few short vectors"):
            act.dma_start(wif[:], w_in[0, :, 2048:2056].rearrange("(k p) c -> p k c", p=P)).then_inc(s.wif_in, 16)
            act.dma_start(gate_bias[:, 0:1], b_i.rearrange("a h -> h a")).then_inc(s.gb_in, 16)
            act.dma_start(gate_bias[:, 1:2], b_f.rearrange("a h -> h a")).then_inc(s.gb_in, 16)
        for j, v in enumerate((lam_q1, lam_q2, lam_k1, lam_k2)):
            act.dma_start(lamv[:, j, :], v[0].partition_broadcast(P)).then_inc(s.lam_in, 16)
        for k in range(KB):
            act.wait_ge(s.h_full, k + 1)
            act.copy(hi_h[:, k, :], hfull[:, k % 2, :]).then_inc(s.h_hi, 1)
        def split(section, blk, odd):
            for kh in range(2):
                if section == XM:
                    act.wait_ge(raw_in[0][blk // 2], 16)
                elif isinstance(blk, int) and blk == 0:
                    for q in (2 * kh, 2 * kh + 1):
                        act.wait_ge(raw_in[slot_of(section)][q], 16 * lap_of(section))
                act.wait_ge(s.pieces_used, blk * 2 + (PIECES * section + kh + 1))
                b = 2 * odd + kh
                act.copy(whi[:, b, :].rearrange("p (k c) -> p k c", c=P), piece(section, blk, kh)).then_inc(s.hi_ready, 1)

        def evacuate(section, blk, odd):
            if section in (WM, WA):
                return
            act.wait_ge(s.pieces_used, blk * 2 + (PIECES * section + 2 + NBUF))
            src = ps[:, bank(section, odd), :]
            b1 = bass.ds(blk, 1)
            if section == XM:
                act.copy(xm[:, b1, CONV - 1:], src[:, 0:S].unsqueeze(1)).then_inc(evac[XM], 1)
            elif section == OG:
                act.activation(ot[:, b1, :], src[:, 0:T].unsqueeze(1), ACT.Sigmoid).then_inc(evac[OG], 1)
            elif section == KA:
                act.copy(ka[:, b1, :], src[:, 0:S].unsqueeze(1)).then_inc(evac[KA], 1)
            elif section == QA:
                act.mul(qa[0:AD, 0, b1, :], src[0:AD, 0:T].unsqueeze(1), AD ** -0.5)
                act.mul(qa[AD:P, 1, b1, :], src[AD:P, 0:T].unsqueeze(1), AD ** -0.5).then_inc(evac[QA], 1)
            elif section == VA:
                act.copy(vat[:, b1, :], src[:, 0:S].unsqueeze(1)).then_inc(evac[VA], 1)
            else:
                act.activation(sg[:, b1, :], src[:, 0:T].unsqueeze(1), ACT.Sigmoid).then_inc(evac[section], 1)

        def stream(section, following, extra=None):
            if section in (XM, OG, GA, GB, WA):
                for blk in range(KB - 2):
                    split(section, blk + 1, (blk + 1) % 2)
                    evacuate(section, blk, blk % 2)
                    if extra:
                        extra(blk, blk % 2)
            else:
                with act.Fori(0, KB // 2 - 1) as i:
                    for j in range(2):
                        split(section, i * 2 + (j + 1), (j + 1) % 2)
                        evacuate(section, i * 2 + j, j)
                        if extra:
                            extra(i * 2 + j, j)
            split(section, KB - 1, 1)
            evacuate(section, KB - 2, 0)
            if extra:
                extra(KB - 2, 0)
            if following == "out":
                split_out(0)
                split_out(1)
            elif following is not None:
                split(following, 0, 0)
            evacuate(section, KB - 1, 1)
            if extra:
                extra(KB - 1, 1)

        def split_out(n):
            if n % 4 == 0:
                act.wait_ge(raw_in[slot_of("out")][n // 4], 16 * lap_of("out"))
            act.wait_ge(s.pieces_used, OUT_BASE + n + 1)
            act.copy(whi[:, n % NBUF, :], out_piece(n)).then_inc(s.hi_ready, 1)

        def conv_sigmoid(behind, odd):
            blk = behind - 2
            if blk < 0:
                return
            act.wait_ge(s.conv_acc, blk + 1)
            act.wait_ge(s.xc_ready, blk + 1)
            act.activation(csig[:, odd, :], xc[:, bass.ds(blk, 1), :], ACT.Sigmoid).then_inc(s.conv_sig, 1)

        split(XM, 0, 0)
        act.wait_ge(s.wif_in, 16)
        act.wait_ge(s.consts, 1)
        for narrow, wide in ((ident_b, ident), (late_b, late), (ahead_b, ahead)):
            act.copy(narrow[:], wide[:]).then_inc(s.masks_ready, 1)
        act.copy(wif_hi[:, :, 0:MH], wif[:, :, MH:2 * MH]).then_inc(s.wif_split, 1)
        act.copy(wif_hi[:, :, 32:32 + MH], wif[:, :, 0:MH]).then_inc(s.wif_split, 1)


        stream(XM, OG)
        act.wait_ge(s.lam_sum, 1)
        act.activation(lams[:, 2:4], lams[:, 0:2], ACT.Exp).then_inc(s.lam_exp, 1)
        act.wait_ge(s.hres_ready, 1)
        stream(OG, None, conv_sigmoid)
        for odd in range(2):
            conv_sigmoid(KB + odd, odd)

        for g in range(16):
            act.wait_ge(s.hp_done, g + 1)
            if g % 2 == 0:
                act.copy(qm[:, g // 2, :], ps[:, 4 + g % 4, 0:T]).then_inc(s.hp_act, 1)
            else:
                act.mul(km[:, g // 2, :], ps[:, 4 + g % 4, 0:S], MD ** -0.5).then_inc(s.hp_act, 1)
            if g == 3:
                act.wait_ge(s.scan_e, 1)
                act.activation(scan[:, 1, SCAN:], gtmp[:, 1, :], ACT.Exp, scale=-1.0).then_inc(s.act, 1)
                act.wait_ge(s.act, 1)
                act.activation(gtmp[:, 1, :], scan[:, 1, SCAN:], ACT.Ln, bias=1.0).then_inc(s.scan_l, 1)
        act.wait_ge(s.vm_ones, 1)
        for g in range(16, 28):
            h, st = divmod(g - 16, 3)
            n = STILES[st][1]
            act.wait_ge(s.hp_done, g + 1)
            act.copy(vm[0:n, st, h, 0:MD], ps[0:n, 4 + g % 4, 0:MD]).then_inc(s.hp_act, 1)
        act.wait_ge(s.aux_ready, 2)
        act.activation(em_col[:], ps[:, 7, 12:20].rearrange("p (t h) -> p t h", h=MH), ACT.Exp).then_inc(s.exp_ready, 1)
        act.wait_ge(s.aux_ready, 2)
        for h in range(MH):
            act.wait_ge(s.mb_done, h + 1)
            if h >= 2:
                act.wait_ge(s.w_done, h - 1)
            for (c0, n, rows), st in zip(((0, 256, P), (256, 144, P), (400, META, META)), range(3)):
                last = act.activation(ex[0:rows, h % 2, c0:c0 + n], ps[0:rows, 4 + h % 2, c0:c0 + n], ACT.Exp,
                                      bias=at_col[0:rows, st, h:h + 1], scale=-1.0)
            last.then_inc(s.e_done, 1)

        split(KA, 0, 0)
        stream(KA, QA)
        act.wait_ge(s.qa_zero, 2)
        stream(QA, VA)
        stream(VA, None)

        for g in range(6):
            st, half = divmod(g, 2)
            n = STILES[st][1]
            act.wait_ge(s.va_t, g + 1)
            act.copy(va[0:n, st, 512 * half:512 * half + 512], ps[0:n, 4 + g % 4, :]).then_inc(s.va_ready, 1)

        def softmax_exp(h):
            act.wait_ge(s.nmax_done, h + 1)
            if h >= 2:
                act.wait_ge(s.tr_done, h - 1)
                act.wait_ge(s.attn_done, h - 1)
            for t, (c0, n) in ((1, (144, S)), (0, (0, 144))):
                for half in range(2):
                    last = act.activation(ea[:, h % 2, half, c0:c0 + n], ps[:, 4 + 2 * (h % 2) + half, c0:c0 + n],
                                          ACT.Exp, bias=nmax[:, h % 2, t, half:half + 1],
                                          accum_out=rsum[:, h % 2, t, half:half + 1])
                last.then_inc(s.exp_done, 1)

        def squares(h):
            act.wait_ge(s.o_copied, h + 1)
            for t in range(TT):
                if h + t:
                    act.wait_ge(s.o_squared, TT * h + t)
                act.activation(junk[:], oall[:, t, P * h:P * h + P], ACT.Square,
                               accum_out=ssq[:, t * AH + h:t * AH + h + 1]).then_inc(s.o_squared, 1)

        softmax_exp(0)
        for h in range(AH):
            if h + 1 < AH:
                softmax_exp(h + 1)
            if h:
                squares(h - 1)
            act.wait_ge(s.tr_done, h + 1)
            if h >= 1:
                act.wait_ge(s.av_done, h)
            act.copy(att[:], ps[:, 0, 0:3 * P]).then_inc(s.at_act, 1)
        split(GA, 0, 0)
        squares(AH - 1)

        def branch_hi(full, hi_sem, hi):
            def step(blk, odd):
                act.wait_ge(full, blk + 1)
                act.copy(hi[:, bass.ds(blk, 1), :], mtmp[:, odd:odd + 1, :]).then_inc(hi_sem, 1)
            return step

        stream(GA, WM, branch_hi(s.ym_full, s.ym_hi_s, ym_hi))

        stream(WM, GB)
        act.wait_ge(evac[WM], KB + 2)
        stream(GB, WA, branch_hi(s.ya_full, s.ya_hi_s, ya_hi))

        def merged_hi(ahead, odd):
            blk = ahead - 1
            if blk >= 0:
                act.wait_ge(s.merged_s, blk + 3)
                act.copy(mg_hi[:, blk, :], merged[:, blk, :]).then_inc(s.mg_hi_s, 1)

        stream(WA, "out", merged_hi)
        merged_hi(KB, 0)
        for n in range(2, PIECES):
            if n == NBUF:
                act.wait_ge(s.mg_lo_s, KB)
                for j, v in enumerate((ln1_g, ln1_b)):
                    act.dma_start(rows1[:, j, :], v[0].partition_broadcast(P)).then_inc(s.rows1_in, 16)
            split_out(n)

        for k in range(4, KB):
            act.wait_ge(s.h1_t, 2 if k < 6 else 4)
            act.activation(h1t[:, k, :], turned1[:, k, :], ACT.Identity, bias=chan[:, C_L1B + k:C_L1B + k + 1],
                           scale=chan[:, C_L1G + k:C_L1G + k + 1]).then_inc(s.h1t_act, 1)
        act.activation(table_load[:], neglam[0:1, :], ACT.Exp)
        act.wait_ge(s.logit_done, 1)
        act.copy(lgt[:], ps[0:NE, 4, 0:T]).then_inc(s.logit_sb, 1)
        act.wait_ge(s.router_exp, 1)
        for t in range(TT):
            act.activation(rt[:, 1, NE * t:NE * t + NE], rt[:, 0, NE * t:NE * t + NE], ACT.Exp,
                           bias=rt[:, 15, t:t + 1], accum_out=rt[:, 15, 4 + t:5 + t]).then_inc(s.exp_r, 1)
        act.wait_ge(s.h1_ready, 1)
        for t in range(TT):
            act.mul(acc[:, t, :], h1[:, t, :], ALPHA).then_inc(s.acc_ready, 1)
        for j, v in enumerate((ln2_g, ln2_b)):
            act.dma_start(rows1[:, j, :], v[0].partition_broadcast(P)).then_inc(s.rows2_in, 16)

        act.wait_ge(s.units_ready, 1)
        count = act.value_load(total[:], min_val=NE, max_val=UNITS - 2)
        with act.Fori(0, count) as u:
            for half in range(2):
                act.wait_ge(s.gate_used, u * 4 + 4)
                act.copy(gsb[:, 512 * half:512 * half + 512], ps[:, half, :]).then_inc(s.gsb_ready, 1)
            for half in range(2):
                act.wait_ge(s.up_used, u * 4 + 4)
                act.copy(usb[:, 512 * half:512 * half + 512], ps[:, 2 + half, :]).then_inc(s.usb_ready, 1)
            act.wait_ge(s.gate_ready, u + 1)
            act.activation(gsig[:], gate[:], ACT.Sigmoid).then_inc(s.gsig_ready, 1)
            for half in range(2):
                act.wait_ge(s.down_used, u * 4 + 4)
                act.copy(zsb[:, 512 * half:512 * half + 512], ps[:, 6 + half, :]).then_inc(s.z_ready, 1)

    @block.vector
    def _(dve):
        own = Steps(dve, s.dve)
        for j, n in enumerate((META, P, P)):
            dve.wait_ge((s.x_in0, s.x_in1, s.x_in2)[j], 16)
            for c in range(2):
                own(dve.bn_stats(stats[0:n, j, c, :], xt[0:n, j, 512 * c:512 * c + 512]))
        own.settle()
        for j, n in enumerate((META, P, P)):
            own(dve.bn_aggr(mv[0:n, j, :], stats[0:n, j, :, :]))
        own.settle()
        for j, n in enumerate((META, P, P)):
            dve.tensor_scalar(ve[0:n, j:j + 1], mv[0:n, j, 1:2], EPS, None, ALU.add).then_inc(s.var_ready, 1)
        dve.wait_ge(s.rstd_ready, 2)
        for j, n in enumerate((META, P, P)):
            dve.tensor_scalar(xt[0:n, j, :], xt[0:n, j, :], mv[0:n, j, 0:1], rstd[0:n, j:j + 1],
                              ALU.subtract, ALU.mult).then_inc(s.xn_ready, 1)
        dve.wait_ge(s.rows_t, 1)
        dve.tensor_copy(chan[:], ps[:, 7, 0:81]).then_inc(s.chan_ready, 1)
        dve.wait_ge(s.chan_ready, 1)
        own(dve.tensor_scalar(chan[:, C_AG:C_AG + 1], chan[:, C_AG:C_AG + 1], 1.0 - LAM_INIT, None, ALU.mult))


        def low_half(k):
            dve.wait_ge(s.h_hi, k + 1)
            dve.tensor_tensor(lo_h[:, k, :], hfull[:, k % 2, :], hi_h[:, k, :].bitcast(F32),
                              ALU.subtract).then_inc(s.h_lo, 1)

        for k in range(KB):
            dve.wait_ge(s.ht_t, k + 1)
            if k >= 2:
                dve.wait_ge(s.h_lo, k - 1)
            dve.tensor_scalar(hfull[:, k % 2, :], ps[:, k % 4, 0:S], chan[:, C_LNG + k:C_LNG + k + 1],
                              chan[:, C_LNB + k:C_LNB + k + 1], ALU.mult, ALU.add).then_inc(s.h_full, 1)
            if k:
                low_half(k - 1)
        low_half(KB - 1)
        def split(section, blk, odd):
            for kh in range(2):
                b = 2 * odd + kh
                dve.wait_ge(s.hi_ready, blk * 2 + (PIECES * section + kh + 1))
                dve.tensor_tensor(wlo[:, b, :].rearrange("p (k c) -> p k c", c=P), piece(section, blk, kh),
                                  whi[:, b, :].bitcast(F32).rearrange("p (k c) -> p k c", c=P),
                                  ALU.subtract).then_inc(s.lo_ready, 1)

        def evacuate(section, blk, odd):
            if section not in (WM, WA):
                return
            dve.wait_ge(s.pieces_used, blk * 2 + (PIECES * section + 2 + NBUF))
            src = ps[:, bank(section, odd), 0:T].unsqueeze(1)
            b1 = bass.ds(blk, 1)
            if section == WM:
                dve.tensor_tensor(merged[:, b1, :], src, sg[:, b1, :], ALU.mult).then_inc(evac[WM], 1)
            else:
                dve.wait_ge(s.merged_s, blk + 1)
                dve.tensor_tensor(mtmp[:, odd:odd + 1, :], src, sg[:, b1, :], ALU.mult).then_inc(evac[WA], 1)
                dve.wait_ge(evac[WA], blk + 3)
                dve.tensor_tensor(merged[:, b1, :], mtmp[:, odd:odd + 1, :], merged[:, b1, :],
                                  ALU.add).then_inc(s.merged_s, 1)

        def stream(section, following, extra=None, per=0, ahead_of=None):
            n0 = own.n
            if section == WA:
                for blk in range(KB - 2):
                    split(section, blk + 1, (blk + 1) % 2)
                    evacuate(section, blk, blk % 2)
                    extra(blk, blk % 2)
            else:
                with dve.Fori(0, KB // 2 - 1) as i:
                    own.base = i * (2 * per)
                    for j in range(2):
                        if ahead_of:
                            ahead_of(i * 2 + j, j)
                        split(section, i * 2 + (j + 1), (j + 1) % 2)
                        evacuate(section, i * 2 + j, j)
                        if extra:
                            extra(i * 2 + j, j)
                assert own.n == n0 + 2 * per
                own.base = 0
                own.n = n0 + (KB - 2) * per
            if ahead_of:
                ahead_of(KB - 2, 0)
            split(section, KB - 1, 1)
            evacuate(section, KB - 2, 0)
            if extra:
                extra(KB - 2, 0)
            if ahead_of:
                ahead_of(KB - 1, 1)
            if following == "out":
                split_out(0)
                split_out(1)
            elif following is not None:
                split(following, 0, 0)
            evacuate(section, KB - 1, 1)
            if extra:
                extra(KB - 1, 1)

        def split_out(n):
            dve.wait_ge(s.hi_ready, OUT_BASE + n + 1)
            dve.tensor_tensor(wlo[:, n % NBUF, :], out_piece(n), whi[:, n % NBUF, :].bitcast(F32),
                              ALU.subtract).then_inc(s.lo_ready, 1)

        def conv(last_blk, odd):
            if not odd:
                return
            pair = [last_blk - 1 if isinstance(last_blk, int) else dve.snap(last_blk - 1), last_blk]
            for blk in pair:
                own(dve.tensor_scalar(xc[:, bass.ds(blk, 1), :], xm[:, bass.ds(blk, 1), 0:S], c_conv(0, blk),
                                      chan[:, bass.ds(blk + C_CONVB, 1)], ALU.mult, ALU.add))
            for w in range(1, CONV):
                for b, blk in enumerate(pair):
                    dve.wait_ge(s.dve, own.base + own.n - 1 + (w == CONV - 1 and b == 1))
                    ins = dve.scalar_tensor_tensor(out=xc[:, bass.ds(blk, 1), :], in0=xm[:, bass.ds(blk, 1), w:w + S],
                                                   scalar=c_conv(w, blk), in1=xc[:, bass.ds(blk, 1), :],
                                                   op0=ALU.mult, op1=ALU.add)
                    if w < CONV - 1:
                        own(ins)
                    else:
                        ins.then_inc(s.conv_acc, 1)

        split(XM, 0, 0)
        dve.wait_ge(s.wif_split, 2)
        for a, b in ((0, MH), (32, 0)):
            own(dve.tensor_tensor(wif_lo[:, :, a:a + MH], wif[:, :, b:b + MH],
                                  wif_hi[:, :, a:a + MH].bitcast(F32), ALU.subtract))
        own.settle()
        dve.sem_inc(s.wif_split, 1)
        dve.wait_ge(s.lam_in, 64)
        own(dve.tensor_tensor(lamp[:], lamv[:, 0:2, :], lamv[:, 2:4, :], ALU.mult))
        own.settle()
        dve.tensor_reduce(lams[:, 0:2], lamp[:], AX.X, ALU.add).then_inc(s.lam_sum, 1)


        stream(XM, OG)
        dve.wait_ge(evac[XM], KB + 2)
        stream(OG, None, conv, per=CONV - 1)

        dve.wait_ge(s.lam_exp, 1)
        own(dve.tensor_tensor(neglam[:], lams[:, 3:4], lams[:, 2:3], ALU.subtract))
        own.settle()
        own(dve.tensor_scalar(neglam[:], neglam[:], -LAM_INIT, None, ALU.add))
        dve.wait_ge(s.gb_in, 32)
        dve.wait_ge(s.if_done, 1)
        own(dve.memset(scan[:, :, 0:SCAN], 0.0))
        own(dve.tensor_scalar(gtmp[:, 0, :], ps[0:MH, 0, 0:S], gate_bias[:, 1:2], None, ALU.add))
        own(dve.tensor_copy(scan[:, 2, SCAN:], ps[32:32 + MH, 0, 0:S]))
        own.settle()
        dve.scalar_tensor_tensor(out=gtmp[:, 1, :], in0=gtmp[:, 0, :], scalar=-1.0, in1=gtmp[:, 0, :],
                                 op0=ALU.mult, op1=ALU.max).then_inc(s.scan_e, 1)
        own(dve.tensor_scalar(gtmp[:, 0, :], gtmp[:, 0, :], 0.0, None, ALU.min))
        dve.wait_ge(s.scan_l, 1)
        own.settle()
        own(dve.tensor_tensor(scan[:, 0, SCAN:], gtmp[:, 0, :], gtmp[:, 1, :], ALU.subtract))
        own.settle()

        def prefix(src, dst, op):
            step = 1
            while step < S:
                own(dve.tensor_tensor(scan[:, dst, SCAN:], scan[:, src, SCAN:],
                                      scan[:, src, SCAN - step:SCAN - step + S], op))
                own.settle()
                src, dst, step = dst, src, 2 * step
            return src

        b_at = prefix(0, 1, ALU.add)
        own(dve.scalar_tensor_tensor(out=gtmp[:, 0, :], in0=scan[:, 2, SCAN:], scalar=gate_bias[:, 0:1],
                                     in1=scan[:, b_at, SCAN:], op0=ALU.add, op1=ALU.subtract))
        own.settle()
        own(dve.tensor_copy(scan[:, 2, SCAN:], gtmp[:, 0, :]))
        own.settle()
        m_at = prefix(2, 1 - b_at, ALU.max)
        own(dve.tensor_scalar(mrow[:], scan[:, m_at, SCAN:], 0.0, None, ALU.max))
        own.settle()
        dve.scalar_tensor_tensor(out=gtmp[:, 1, :], in0=scan[:, b_at, SCAN:], scalar=-1.0, in1=mrow[:],
                                 op0=ALU.mult, op1=ALU.subtract).then_inc(s.gates_ready, 1)
        dve.wait_ge(s.gates_t, 1)
        dve.tensor_copy(at_col[:, 0:2, :], ps[:, 7, 0:8].rearrange("p (t h) -> p t h", h=MH)).then_inc(s.aux_ready, 1)
        dve.tensor_copy(at_col[0:META, 2, :], ps[0:META, 7, 8:12]).then_inc(s.aux_ready, 1)
        for g in range(4):
            t, half = divmod(g, 2)
            dve.wait_ge(s.ot_t, g + 1)
            dve.tensor_copy(hh[:, t, 512 * half:512 * half + 512], ps[:, g, :]).then_inc(s.ot_ready, 1)

        def weights(h):
            dve.wait_ge(s.e_done, h + 1)
            dve.wait_ge(s.sc_done, h + 1)
            if h == 0:
                dve.wait_ge(s.vm_ones, 5)
            if h >= 2:
                dve.wait_ge(s.num_done, h - 1)
            b, e = 6 + h % 2, h % 2
            own(dve.tensor_tensor(wgt[:, e, 0, :], ps[:, b, 0:256], ex[:, e, 0:256], ALU.mult))
            own(dve.tensor_tensor(wgt[:, e, 1, 112:256], ps[:, b, 256:400], ex[:, e, 256:400], ALU.mult))
            dve.tensor_tensor(wgt[0:META, e, 2, 240:256], ps[0:META, b, 400:416], ex[0:META, e, 400:416],
                              ALU.mult).then_inc(s.w_done, 1)

        def outputs(h):
            dve.wait_ge(s.num_done, h + 1)
            dve.wait_ge(s.exp_ready, 1)
            for t in range(TT):
                own(dve.tensor_scalar(den[:, h, t:t + 1], ps[:, 2 * (h % 2) + t, MD:MD + 1], -1.0,
                                      em_col[:, t, h:h + 1], ALU.mult, ALU.max))
            own.settle()
            for t in range(TT):
                own(dve.tensor_tensor(den[:, h, t:t + 1], ps[:, 2 * (h % 2) + t, MD:MD + 1], den[:, h, t:t + 1],
                                      ALU.max))
            own.settle()
            own(dve.reciprocal(rden[:, h, :], den[:, h, :]))
            own.settle()
            for t in range(TT):
                cols = slice(MD * h, MD * h + MD)
                dve.scalar_tensor_tensor(out=hh[:, t, cols], in0=ps[:, 2 * (h % 2) + t, 0:MD],
                                         scalar=rden[:, h, t:t + 1], in1=hh[:, t, cols],
                                         op0=ALU.mult, op1=ALU.mult).then_inc(s.hh_done, 1)

        dve.wait_ge(s.ot_ready, 4)
        weights(0)
        for h in range(MH):
            if h + 1 < MH:
                weights(h + 1)
            else:
                split(KA, 0, 0)
            outputs(h)
        dve.wait_ge(s.hh_done, TT * MH)
        hh8 = hh[:].rearrange("p t (h e) -> p (t h) e", e=MD)

        def head_stats(blk, odd):
            own(dve.bn_stats(stats8[:, bass.ds(blk, 1), :].rearrange("p a b -> p (a b)"),
                             hh8[:, bass.ds(blk, 1), :].rearrange("p a b -> p (a b)")))

        def head_norm(blk, odd):
            h1_ = hh8[:, bass.ds(blk, 1), :].rearrange("p a b -> p (a b)")
            dve.tensor_scalar(h1_, h1_, mv8[:, bass.ds(blk, 1), 0], rstd8[:, bass.ds(blk, 1)],
                              ALU.subtract, ALU.mult).then_inc(s.hn_ready, 1)

        stream(KA, QA, head_stats, per=1)
        own.settle()
        for i in range(TT * MH):
            own(dve.bn_aggr(mv8[:, i, :], stats8[:, i, :]))
        own.settle()
        dve.tensor_scalar(ve8[:], mv8[:, :, 1], EPS, None, ALU.add).then_inc(s.var8, 1)
        dve.wait_ge(s.rstd8_ready, 1)
        stream(QA, VA, head_norm)
        stream(VA, None)

        def row_max(h):
            dve.wait_ge(s.s_done, h + 1)
            b = 4 + 2 * (h % 2)
            for t, (c0, n) in enumerate(((0, 144), (144, S))):
                last = dve.tensor_reduce(nmax[:, h % 2, t, :], ps[:, b:b + 2, c0:c0 + n], AX.X, ALU.max, negate=True)
            last.then_inc(s.nmax_done, 1)

        def combine(h):
            e = h % 2
            for t, (c0, n) in ((1, (144, S)), (0, (0, 144))):
                dve.wait_ge(s.exp_done, 2 * h + 2 - t)
                own(dve.reciprocal(rinv[:, e, t, :], rsum[:, e, t, :]))
                own.settle()
                own(dve.tensor_scalar(rinv[:, e, t, 1:2], rinv[:, e, t, 1:2], neglam[:, 0:1], None, ALU.mult))
                own(dve.tensor_scalar(ea[:, e, 0, c0:c0 + n], ea[:, e, 0, c0:c0 + n], rinv[:, e, t, 0:1], None, ALU.mult))
                own.settle()
                ins = dve.scalar_tensor_tensor(out=ea[:, e, 0, c0:c0 + n], in0=ea[:, e, 1, c0:c0 + n],
                                               scalar=rinv[:, e, t, 1:2], in1=ea[:, e, 0, c0:c0 + n],
                                               op0=ALU.mult, op1=ALU.add)
                if t == 0:
                    ins.then_inc(s.attn_done, 1)
                else:
                    own(ins)

        def take_output(h):
            dve.wait_ge(s.av_done, h + 1)
            dve.tensor_copy(oall[:, :, P * h:P * h + P],
                            ps[:, 2 + h % 2, 0:2 * P].rearrange("p (t v) -> p t v", v=P)).then_inc(s.o_copied, 1)

        row_max(0)
        for h in range(AH):
            combine(h)
            if h + 1 < AH:
                row_max(h + 1)
            if h:
                take_output(h - 1)
            dve.wait_ge(s.tr_done, h + 1)
            dve.tensor_copy(att2[:], ps[0:META, 1, 0:2 * P]).then_inc(s.at_dve, 1)
        split(GA, 0, 0)
        take_output(AH - 1)
        o4 = oall[:].rearrange("p t (h v) -> p (t h) v", v=AV)

        def output_norm(blk, odd):
            two = bass.ds(blk * 2, 2)
            dve.wait_ge(s.rstda_ready, 1)
            dve.tensor_tensor(o4[:, two, :], o4[:, two, :], rstda[:, two].unsqueeze(2).to_broadcast([P, 2, AV]),
                              ALU.mult).then_inc(s.ya_ready, 1)

        def branch(full, hi_sem, lo_sem, hi, lo, gain):
            def scale(blk, odd):
                dve.wait_ge(lo_sem, blk + 1)
                dve.tensor_scalar(mtmp[:, odd:odd + 1, :], turned[:, bass.ds(blk, 1), :], gain(blk), None,
                                  ALU.mult).then_inc(full, 1)

            def low(blk, odd):
                dve.wait_ge(hi_sem, blk + 1)
                b1 = bass.ds(blk, 1)
                dve.tensor_tensor(lo[:, b1, :], mtmp[:, odd:odd + 1, :], hi[:, b1, :].bitcast(F32),
                                  ALU.subtract).then_inc(lo_sem, 1)

            dve.sem_inc(lo_sem, 2)
            return scale, low

        turned = ps[:, 4:8, :].rearrange("p a (b c) -> p (a b) c", c=T)
        dve.wait_ge(s.ym_t, 1)
        scale, low = branch(s.ym_full, s.ym_hi_s, s.ym_lo_s, ym_hi, ym_lo,
                            lambda blk: chan[:, bass.ds(blk + C_MG, 1)])
        dve.wait_ge(s.o_squared, TT * AH)
        dve.tensor_scalar(vea[:], ssq[:], 1.0 / AV, EPS, ALU.mult, ALU.add).then_inc(s.vara, 1)
        dve.wait_ge(s.o_copied, AH)

        def norm_and_low(blk, odd):
            output_norm(blk, odd)
            low(blk, odd)

        stream(GA, WM, norm_and_low, ahead_of=scale)
        stream(WM, GB)
        dve.wait_ge(s.ya_t, 1)
        scale, low = branch(s.ya_full, s.ya_hi_s, s.ya_lo_s, ya_hi, ya_lo, lambda blk: chan[:, C_AG:C_AG + 1])
        stream(GB, WA, low, ahead_of=scale)
        def merged_lo(ahead, odd):
            blk = ahead - 1
            if blk >= 0:
                dve.wait_ge(s.mg_hi_s, blk + 1)
                dve.tensor_tensor(mg_lo[:, blk, :], merged[:, blk, :], mg_hi[:, blk, :].bitcast(F32),
                                  ALU.subtract).then_inc(s.mg_lo_s, 1)

        dve.wait_ge(s.ya_lo_s, KB + 2)
        dve.sem_inc(s.merged_s, 2)
        stream(WA, "out", merged_lo)
        merged_lo(KB, 0)
        for n in range(2, PIECES):
            split_out(n)

        def variance(t, buf, summed, ready):
            for c in range(2):
                dve.wait_ge(*summed(c))
                own(dve.bn_stats(stats[:, t, c, :], buf[:, t, 512 * c:512 * c + 512]))
            own.settle()
            own(dve.bn_aggr(mv[:, t, :], stats[:, t, :, :]))
            own.settle()
            dve.tensor_scalar(ve[:, t:t + 1], mv[:, t, 1:2], EPS, None, ALU.add).then_inc(ready, 1)

        dve.wait_ge(s.pieces_used, OUT_BASE + PIECES + NBUF)
        dve.wait_ge(s.hres_ready, 1)
        for t in range(TT):
            for c in range(2):
                dve.scalar_tensor_tensor(out=h1[:, t, 512 * c:512 * c + 512],
                                         in0=hres[:, t, 512 * c:512 * c + 512], scalar=ALPHA,
                                         in1=ps[:, 4 + 2 * t + c, :], op0=ALU.mult,
                                         op1=ALU.add).then_inc(s.resid_done, 1)
            variance(t, h1, lambda c: (s.resid_done, 2 * t + c + 1), s.var1)
        for t in range(TT):
            dve.wait_ge(s.rstd1, t + 1)
            dve.tensor_scalar(h1[:, t, :], h1[:, t, :], mv[:, t, 0:1], rstd[:, t:t + 1],
                              ALU.subtract, ALU.mult).then_inc(s.xn1_ready, 1)
        for k in range(4):
            dve.wait_ge(s.h1_t, 1 if k < 2 else 3)
            dve.tensor_scalar(h1t[:, k, :], turned1[:, k, :], chan[:, C_L1G + k:C_L1G + k + 1],
                              chan[:, C_L1B + k:C_L1B + k + 1], ALU.mult, ALU.add).then_inc(s.h1t_dve, 1)

        def val(r):
            return rt[:, r, :].rearrange("p (t e) -> p t e", e=NE)

        def grp(r):
            return rt[:, r, :].rearrange("p (t g i) -> p t g i", g=NG, i=EPG)

        def first_max(src, r_eq, r_key, r_one, out_row, groups):
            n = NG if groups else NE
            rank = rank16[:, NE - n:NE].unsqueeze(1).to_broadcast([P, TT, n])
            own(dve.tensor_reduce(r_one, src, AX.X, ALU.max))
            own.settle()
            own(dve.tensor_tensor(r_eq, src, r_one.unsqueeze(2).to_broadcast([P, TT, n]), ALU.is_equal))
            own.settle()
            own(dve.tensor_tensor(r_key, r_eq, rank, ALU.mult))
            own.settle()
            own(dve.tensor_reduce(r_one, r_key, AX.X, ALU.max))
            own.settle()
            own(dve.tensor_tensor(out_row, r_key, r_one.unsqueeze(2).to_broadcast([P, TT, n]), ALU.is_equal))
            own.settle()

        def load_unit(u):
            return (dve.value_load(unit_of[0:1, 0, bass.ds(u, 1)], min_val=0, max_val=NE - 1),
                    dve.value_load(unit_of[0:1, 1, bass.ds(u, 1)], min_val=0, max_val=MAXBLK - 1))

        def pick_tokens(e, b):
            for t in range(TT):
                dve.tensor_scalar(pick[:, t, :], slotno[:].rearrange("p a b -> p (a b)"), boff[:, bass.ds(b, 1)],
                                  slot[:, t, bass.ds(e, 1)], ALU.add, ALU.is_equal).then_inc(s.pick_ready, 1)

        def weigh(e):
            for t in range(TT):
                dve.tensor_scalar(wpick[:, t, :], pick[:, t, :], comb[:, t, bass.ds(e, 1)], None,
                                  ALU.mult).then_inc(s.wpick_ready, 1)

        def take_gathered():
            dve.tensor_copy(xg[:], ps[:, 0:2, :].rearrange("p a (k c) -> p (a k) c", c=P)[:, :, 0:SLOTS]
                            ).then_inc(s.xg_ready, 1)

        dve.wait_ge(s.logit_t, 1)
        own(dve.tensor_copy(val(0), ps[:, 5, 0:TT * NE].rearrange("p (t e) -> p t e", e=NE)))
        own.settle()
        dve.tensor_reduce(rt[:, 15, 0:TT], val(0), AX.X, ALU.max, negate=True).then_inc(s.router_exp, 1)
        dve.wait_ge(s.exp_r, TT)

        own(dve.reciprocal(rt[:, 15, 8:8 + TT], rt[:, 15, 4:4 + TT]))
        own.settle()
        own(dve.tensor_tensor(val(2), val(1), rt[:, 15, 8:8 + TT].unsqueeze(2).to_broadcast([P, TT, NE]), ALU.mult))
        own.settle()
        dve.wait_ge(s.rb_in, 16)
        own(dve.tensor_tensor(val(3), val(2), rbias[:].unsqueeze(1).to_broadcast([P, TT, NE]), ALU.add))
        own.settle()
        g8 = rt[:, 4, 0:TT * NG].rearrange("p (t g) -> p t g", g=NG)
        e8 = rt[:, 5, 0:TT * NG].rearrange("p (t g) -> p t g", g=NG)
        k8 = rt[:, 6, 0:TT * NG].rearrange("p (t g) -> p t g", g=NG)
        own(dve.tensor_reduce(g8, grp(3), AX.X, ALU.max))
        own.settle()
        first_max(g8, e8, k8, rt[:, 15, 12:12 + TT], g8, True)
        own(dve.tensor_scalar(g8, g8, BIG, -BIG, ALU.mult, ALU.add))
        own.settle()
        own(dve.tensor_tensor(grp(3), grp(3), rt[:, 4, 0:TT * NG].rearrange("p (t g) -> p t g", g=NG).unsqueeze(3)
                              .to_broadcast([P, TT, NG, EPG]), ALU.add))
        own.settle()
        first_max(val(3), val(5), val(6), rt[:, 15, 16:16 + TT], val(7), False)
        own(dve.scalar_tensor_tensor(out=val(3), in0=val(7), scalar=-3.0 * BIG, in1=val(3), op0=ALU.mult, op1=ALU.add))
        own.settle()
        first_max(val(3), val(5), val(6), rt[:, 15, 20:20 + TT], val(8), False)
        dve.tensor_tensor(mask[:], val(7), val(8), ALU.add).then_inc(s.mask_ready, 1)
        dve.wait_ge(s.mask_ready, 1)
        own(dve.tensor_tensor(val(9), mask[:], val(2), ALU.mult))
        own.settle()
        own(dve.tensor_reduce(rt[:, 15, 24:24 + TT], val(9), AX.X, ALU.add))
        own.settle()
        own(dve.reciprocal(rt[:, 15, 28:28 + TT], rt[:, 15, 24:24 + TT]))
        own(dve.memset(ends_f[:], 0.0))
        dve.wait_ge(s.rank_done, 1)
        own(dve.scalar_tensor_tensor(out=slot[:], in0=ps[:, 6, 0:TT * NE].rearrange("p (t e) -> p t e", e=NE),
                                     scalar=1.0, in1=mask[:], op0=ALU.add, op1=ALU.mult))
        own(dve.tensor_copy(counts[:], ps[0:1, 6, 2 * NE:3 * NE]))
        own.settle()
        own(dve.tensor_scalar(slot[:], slot[:], -1.0, None, ALU.add))
        own.settle()
        pick_tokens(0, 0)
        own(dve.tensor_tensor(comb[:], val(9), rt[:, 15, 28:28 + TT].unsqueeze(2).to_broadcast([P, TT, NE]), ALU.mult))
        own(dve.tensor_scalar(nblk_f[:], counts[:], float(SLOTS), 1.0, ALU.is_gt, ALU.add))
        own.settle()
        for c in (2, 3):
            own(dve.scalar_tensor_tensor(out=nblk_f[:], in0=counts[:], scalar=float(c * SLOTS), in1=nblk_f[:],
                                         op0=ALU.is_gt, op1=ALU.add))
            own.settle()
        own(dve.tensor_copy(ends_f[:, 0, 32:], nblk_f[:]))
        own.settle()
        src = 0
        for step in (1, 2, 4, 8):
            own(dve.tensor_tensor(ends_f[:, 1 - src, 32:], ends_f[:, src, 32:], ends_f[:, src, 32 - step:32 - step + NE],
                                  ALU.add))
            own.settle()
            src = 1 - src
        own(dve.tensor_copy(blocks[:, 0, :], nblk_f[:]))
        own(dve.tensor_tensor(ends_f[:, 1 - src, 32:], ends_f[:, src, 32:], nblk_f[:], ALU.subtract))
        own(dve.tensor_scalar(blocks[:, 2, :], ends_f[:, src, 32:], -1.0, None, ALU.add))
        own(dve.tensor_copy(total[:], ends_f[:, src, 32 + NE - 1:32 + NE]))
        own.settle()
        dve.tensor_copy(blocks[:, 1, :], ends_f[:, 1 - src, 32:]).then_inc(s.units_ready, 1)
        dve.wait_ge(s.gath_done, 1)
        take_gathered()
        dve.wait_ge(s.pick_ready, TT)
        weigh(0)
        every = unitno[:].unsqueeze(2).to_broadcast([1, UNITS, NE])
        own(dve.tensor_tensor(passed[:], every, ends_f[:, src, 32:].unsqueeze(1).to_broadcast([1, UNITS, NE]), ALU.is_ge))
        own.settle()
        own(dve.tensor_reduce(unit_f[:, 0, :], passed[:], AX.X, ALU.add))
        own.settle()
        own(dve.tensor_tensor(passed[:], passed[:], nblk_f[:].unsqueeze(1).to_broadcast([1, UNITS, NE]), ALU.mult))
        own.settle()
        own(dve.tensor_reduce(unit_f[:, 1, :], passed[:], AX.X, ALU.add))
        own.settle()
        own(dve.tensor_tensor(unit_f[:, 1, :], unitno[:], unit_f[:, 1, :], ALU.subtract))
        own(dve.tensor_scalar(unit_of[:, 0, :], unit_f[:, 0, :], float(NE - 1), None, ALU.min))
        own.settle()
        own(dve.tensor_scalar(unit_of[:, 1, :], unit_f[:, 1, :], float(MAXBLK - 1), None, ALU.min))
        own.settle()

        e1, b1 = load_unit(1)
        dve.wait_ge(s.wpick_ready, TT)
        pick_tokens(e1, b1)
        dve.wait_ge(s.acc_ready, TT)
        count = dve.value_load(total[:], min_val=NE, max_val=UNITS - 2)
        with dve.Fori(0, count) as u:
            dve.wait_ge(s.tg_done, u + 1)
            dve.tensor_reduce(gate[:], ps[:, 4:6, :].rearrange("p a (k h s) -> p (a k) s h", h=2, s=SLOTS), AX.X,
                              ALU.add).then_inc(s.gate_ready, 1)
            dve.wait_ge(s.gsig_ready, u + 1)
            dve.wait_ge(s.gate_ready, u + 1)
            dve.tensor_tensor(gate[:], gate[:], gsig[:], ALU.mult).then_inc(s.moe_dve, 1)
            dve.wait_ge(s.tu_done, u + 1)
            dve.tensor_reduce(upv[:], ps[:, 6:8, :].rearrange("p a (k h s) -> p (a k) s h", h=2, s=SLOTS), AX.X,
                              ALU.add).then_inc(s.moe_dve, 1)
            dve.wait_ge(s.moe_dve, u * 2 + 2)
            dve.tensor_tensor(hid[:], gate[:], upv[:], ALU.mult).then_inc(s.hid_ready, 1)
            for j in range(4):
                t, c = divmod(j, 2)
                cols = slice(512 * c, 512 * c + 512)
                dve.wait_ge(s.scat_done, u * 4 + (j + 1))
                dve.tensor_tensor(acc[:, t, cols], ps[:, 2 + j, :], acc[:, t, cols], ALU.add).then_inc(s.acc_added, 1)
            dve.wait_ge(s.wpt_t, u + 1)
            dve.tensor_copy(wpt[:], ps[:, 0, 0:2 * P].rearrange("p (t c) -> p t c", c=P)).then_inc(s.wpt_ready, 1)
            e1 = dve.value_load(unit_of[0:1, 0, bass.ds(u + 1, 1)], min_val=0, max_val=NE - 1)
            dve.wait_ge(s.pick_ready, u * 2 + 4)
            weigh(e1)
            e2, b2 = load_unit(u + 2)
            dve.wait_ge(s.wpick_ready, u * 2 + 4)
            dve.wait_ge(s.gath_done, u + 2)
            take_gathered()
            pick_tokens(e2, b2)
        for t in range(TT):
            for c in range(2):
                cols = slice(512 * c, 512 * c + 512)
                dve.wait_ge(s.scat_done, count * 4 + (2 * t + c + 1))
                dve.tensor_tensor(acc[:, t, cols], ps[:, 2 + 2 * t + c, :], acc[:, t, cols],
                                  ALU.add).then_inc(s.acc_added, 1)
            variance(t, acc, lambda c: (s.acc_added, count * 4 + (2 * t + c + 5)), s.fin_var)
        dve.wait_ge(s.rows2_in, 32)
        for t in range(TT):
            own(dve.scalar_tensor_tensor(out=acc[:, t, :], in0=acc[:, t, :], scalar=mv[:, t, 0:1],
                                         in1=rows1[:, 0, :], op0=ALU.subtract, op1=ALU.mult))
            dve.wait_ge(s.fin_rstd, t + 1)
            own.settle()
            dve.scalar_tensor_tensor(out=acc[:, t, :], in0=acc[:, t, :], scalar=rstd[:, t:t + 1],
                                     in1=rows1[:, 1, :], op0=ALU.mult, op1=ALU.add).then_inc(s.fin_ready, 1)

    @block.tensor
    def _(pe):
        mm = pe.matmul
        pe.sem_inc(s.pieces_used, NBUF)

        def keep_warm(bank_no, n):
            for _ in range(n):
                mm(ps[:, bank_no, 0:P], ident[:], ident[:], start=True, stop=True)

        pe.wait_ge(s.consts, 1)
        pe.wait_ge(s.crow_in, 128)
        pe.transpose(ps[:, 7, 0:81], crow[:], ident[0:81, 0:81]).then_inc(s.rows_t, 1)
        pe.wait_ge(s.xn_ready, 3)
        for k in range(KB):
            if k >= 4:
                pe.wait_ge(s.h_full, k - 3)
            c = slice(P * k, P * k + P)
            pe.transpose(ps[:, k % 4, 0:META], xt[0:META, 0, c], ident[0:META, 0:META])
            pe.transpose(ps[:, k % 4, META:META + P], xt[:, 1, c], ident[:])
            pe.transpose(ps[:, k % 4, META + P:S], xt[:, 2, c], ident[:]).then_inc(s.ht_t, 1)
        keep_warm(7, 16)
        pe.wait_ge(s.h_lo, KB)

        def stream(section, hi, lo, c0, before_sem):
            n = S - c0 if section in (XM, OG, KA, QA, VA, GA, GB) else T
            if before_sem is not None:
                pe.wait_ge(*before_sem)
            pe.sem_inc(evac[section], 2)
            with pe.Fori(0, KB // 2) as i:
                for j in range(2):
                    o = ps[:, bank(section, j), 0:n]
                    pe.wait_ge(evac[section], i * 2 + (j + 1))
                    for kh in range(2):
                        b = 2 * j + kh
                        pe.wait_ge(s.lo_ready, i * 4 + (PIECES * section + 2 * j + kh + 1))
                        for kk in range(4):
                            k = 4 * kh + kk
                            w1, w2 = whi[:, b, P * kk:P * kk + P], wlo[:, b, P * kk:P * kk + P]
                            mm(o, w1, hi[:, k, c0:c0 + n], start=(k == 0), stop=False)
                            mm(o, w1, lo[:, k, c0:c0 + n], start=False, stop=False)
                            last = mm(o, w2, hi[:, k, c0:c0 + n], start=False, stop=(k == KB - 1))
                        last.then_inc(s.pieces_used, 1)

        stream(XM, hi_h, lo_h, 0, None)
        stream(OG, hi_h, lo_h, META, None)
        pe.wait_ge(s.wif_split, 3)
        pe.wait_ge(evac[XM], KB + 2)
        o = ps[0:64, 0, 0:S]
        for k in range(KB):
            for n, (w, m) in enumerate(((wif_hi, hi_h), (wif_hi, lo_h), (wif_lo, hi_h))):
                last = mm(o, w[:, k, :], m[:, k, :], start=(k == 0 and n == 0), stop=(k == KB - 1 and n == 2))
        last.then_inc(s.if_done, 1)

        hw = raw[:, slot_of("heads"), :, :].rearrange("p a (b e) -> p (a b) e", e=MD)
        pe.wait_ge(s.heads_in, 48)
        pe.wait_ge(s.xc_ready, KB + 2)
        for g in range(28):
            if g >= 4:
                pe.wait_ge(s.hp_act, g - 3)
            for c in range(2):
                if g < 16:
                    h, eb = divmod(g // 2, 2)
                    w = hw[:, 8 * (g % 2) + 2 * h + c, P * eb:P * eb + P]
                    c0 = META if g % 2 == 0 else 0
                    last = mm(ps[:, 4 + g % 4, 0:S - c0], w, xc[:, 2 * h + c, c0:S], start=(c == 0), stop=(c == 1))
                else:
                    h, st = divmod(g - 16, 3)
                    s0, n = STILES[st]
                    last = mm(ps[0:n, 4 + g % 4, 0:MD], xm[:, 2 * h + c, CONV - 1 + s0:CONV - 1 + s0 + n],
                              hw[:, 16 + 2 * h + c, :], start=(c == 0), stop=(c == 1))
            last.then_inc(s.hp_done, 1)

        pe.wait_ge(s.gates_ready, 1)
        pe.wait_ge(s.hp_act, 28)
        for st, (s0, n) in enumerate(STILES):
            pe.transpose(ps[0:n, 7, MH * st:MH * st + MH], gtmp[:, 0, s0:s0 + n], ident[0:MH, 0:MH])
        for t in range(TT):
            last = pe.transpose(ps[:, 7, 12 + MH * t:12 + MH * t + MH], gtmp[:, 1, META + P * t:META + P * t + P],
                                ident[0:MH, 0:MH])
        last.then_inc(s.gates_t, 1)
        pe.wait_ge(evac[OG], KB + 2)
        for g in range(4):
            t, half = divmod(g, 2)
            for k in range(4):
                last = pe.transpose(ps[:, g, P * k:P * k + P], ot[:, 4 * half + k, P * t:P * t + P], ident[:])
            last.then_inc(s.ot_t, 1)

        def scores(h):
            if h == 0:
                pe.wait_ge(s.masks_ready, 3)
                pe.wait_ge(s.aux_ready, 2)
                pe.wait_ge(s.exp_ready, 1)
            if h >= 2:
                pe.wait_ge(s.e_done, h - 1)
            b = 4 + h % 2
            for st, (c0, t0, rows, m0, mn) in enumerate(((0, 0, P, META, 112), (256, 112, P, 0, P),
                                                         (400, 240, META, 0, META))):
                mm(ps[0:rows, b, c0:c0 + T - t0], sel[:, h, 0:rows], mrow[:, META + t0:S], start=True, stop=False,
                   skip_group_check=True)
                last = mm(ps[0:rows, b, c0:c0 + mn], ident_b[0:rows, 0:rows], late_b[0:rows, m0:m0 + mn], start=False,
                          stop=True, skip_group_check=True)
            last.then_inc(s.mb_done, 1)
            if h >= 2:
                pe.wait_ge(s.w_done, h - 1)
            b = 6 + h % 2
            for st, (c0, t0, rows) in enumerate(((0, 0, P), (256, 112, P), (400, 240, META))):
                for c in range(2):
                    last = mm(ps[0:rows, b, c0:c0 + T - t0], km[:, 2 * h + c, STILES[st][0]:STILES[st][0] + rows],
                              qm[:, 2 * h + c, t0:T], start=(c == 0), stop=(c == 1))
            last.then_inc(s.sc_done, 1)

        def numerators(h):
            pe.wait_ge(s.w_done, h + 1)
            if h == 0:
                pe.wait_ge(s.ot_ready, 4)
            if h >= 2:
                pe.wait_ge(s.hh_done, TT * (h - 1))
            for t in range(TT):
                tiles = range(2 + t)
                for st in tiles:
                    n = STILES[st][1]
                    last = mm(ps[:, 2 * (h % 2) + t, 0:MD + 1], wgt[0:n, h % 2, st, P * t:P * t + P],
                              vm[0:n, st, h, :], start=(st == 0), stop=(st == tiles[-1]))
            last.then_inc(s.num_done, 1)

        scores(0)
        for h in range(MH):
            if h + 1 < MH:
                scores(h + 1)
            numerators(h)
        stream(KA, hi_h, lo_h, 0, (s.hh_done, TT * (MH - 1)))
        pe.wait_ge(s.hh_done, TT * MH)
        stream(QA, hi_h, lo_h, META, None)
        stream(VA, hi_h, lo_h, 0, (evac[KA], KB + 2))
        pe.wait_ge(evac[QA], KB + 2)
        pe.wait_ge(evac[VA], KB + 2)
        for g in range(6):
            st, half = divmod(g, 2)
            s0, n = STILES[st]
            if g >= 4:
                pe.wait_ge(s.va_ready, g - 3)
            for k in range(4):
                last = pe.transpose(ps[0:n, 4 + g % 4, P * k:P * k + P], vat[:, 4 * half + k, s0:s0 + n], ident[:])
            last.then_inc(s.va_t, 1)

        def attend(h):
            if h == 0:
                pe.wait_ge(s.va_ready, 6)
            if h >= 2:
                pe.wait_ge(s.exp_done, 2 * (h - 1))
            for half in range(2):
                b = 4 + 2 * (h % 2) + half
                for t, (c0, n) in enumerate(((0, 144), (144, S))):
                    mm(ps[:, b, c0:c0 + n], qa[:, half, h, P * t:P * t + P], ka[:, h, 0:n], start=True, stop=False,
                       skip_group_check=True)
                    last = mm(ps[:, b, c0 + n - P:c0 + n], ident_b[:], ahead_b[:], start=False, stop=True,
                              skip_group_check=True)
            last.then_inc(s.s_done, 1)

        def turn(src, turned):
            for k in range(KB):
                for t in range(TT):
                    c = T * (k % 2) + P * t
                    last = pe.transpose(ps[:, 4 + k // 2, c:c + P], src[:, t, P * k:P * k + P], ident[:])
            last.then_inc(turned, 1)

        attend(0)
        attend(1)
        for h in range(AH):
            e = h % 2
            pe.wait_ge(s.attn_done, h + 1)
            if h >= 1:
                pe.wait_ge(s.at_act, h)
                pe.wait_ge(s.at_dve, h)
            pe.transpose(ps[:, 0, 0:P], ea[:, e, 0, 0:P], ident[:])
            pe.transpose(ps[:, 0, P:2 * P], ea[:, e, 0, 144:144 + P], ident[:])
            pe.transpose(ps[:, 0, 2 * P:3 * P], ea[:, e, 0, 144 + P:144 + 2 * P], ident[:])
            pe.transpose(ps[0:META, 1, 0:P], ea[:, e, 0, P:P + META], ident[:])
            pe.transpose(ps[0:META, 1, P:2 * P], ea[:, e, 0, 144 + 2 * P:144 + S], ident[:]).then_inc(s.tr_done, 1)
            if h + 2 < AH:
                attend(h + 2)
            if h == AH - 1:
                pe.wait_ge(s.exp_done, 2 * AH)
                pe.wait_ge(s.hn_ready, TT * MH)
                turn(hh, s.ym_t)
            pe.wait_ge(s.at_act, h + 1)
            pe.wait_ge(s.at_dve, h + 1)
            if h >= 2:
                pe.wait_ge(s.o_copied, h - 1)
            c = slice(P * h, P * h + P)
            b = 2 + h % 2
            mm(ps[:, b, 0:P], att[:, 0:P], va[:, 0, c], start=True, stop=False, skip_group_check=True)
            mm(ps[:, b, 0:P], att2[:, 0:P], va[0:META, 1, c], start=False, stop=True, skip_group_check=True)
            mm(ps[:, b, P:2 * P], att[:, P:2 * P], va[:, 0, c], start=True, stop=False, skip_group_check=True)
            mm(ps[:, b, P:2 * P], att[:, 2 * P:3 * P], va[:, 1, c], start=False, stop=False, skip_group_check=True)
            mm(ps[:, b, P:2 * P], att2[:, P:2 * P], va[0:META, 2, c], start=False, stop=True,
               skip_group_check=True).then_inc(s.av_done, 1)
        stream(GA, hi_h, lo_h, META, (s.o_copied, AH))
        pe.wait_ge(s.ym_full, KB)
        pe.wait_ge(s.ya_ready, KB)
        turn(oall, s.ya_t)
        pe.wait_ge(s.ym_lo_s, KB + 2)
        stream(WM, ym_hi, ym_lo, 0, (evac[GA], KB + 2))
        stream(GB, hi_h, lo_h, META, None)
        pe.wait_ge(s.ya_lo_s, KB + 2)
        stream(WA, ya_hi, ya_lo, 0, (evac[WM], KB + 2))
        for n in range(PIECES):
            k, half = divmod(n, 2)
            pe.wait_ge(s.mg_lo_s, k + 1)
            pe.wait_ge(s.lo_ready, OUT_BASE + n + 1)
            for t in range(TT):
                o = ps[:, 4 + 2 * t + half, :]
                c = slice(P * t, P * t + P)
                mm(o, mg_hi[:, k, c], whi[:, n % NBUF, :], start=(k == 0), stop=False)
                mm(o, mg_lo[:, k, c], whi[:, n % NBUF, :], start=False, stop=False)
                last = mm(o, mg_hi[:, k, c], wlo[:, n % NBUF, :], start=False, stop=(k == KB - 1))
            last.then_inc(s.pieces_used, 1)

        pe.wait_ge(evac[GB], KB + 2)
        pe.wait_ge(evac[WA], KB + 2)
        keep_warm(0, 26)
        for t in range(TT):
            pe.wait_ge(s.xn1_ready, t + 1)
            for k in (0, 1, 4, 5, 2, 3, 6, 7):
                last = pe.transpose(turned1[:, k, P * t:P * t + P], h1[:, t, P * k:P * k + P], ident[:])
                if t == TT - 1 and k % 2:
                    last.then_inc(s.h1_t, 1)
        pe.wait_ge(s.wr_in, 16)
        pe.wait_ge(s.resid_done, 2 * TT)
        for n, k in enumerate((0, 4, 1, 5, 2, 6, 3, 7)):
            pe.wait_ge(s.h1t_dve if k < 4 else s.h1t_act, k % 4 + 1)
            last = mm(ps[0:NE, 4, 0:T], wr[:, k, :], h1t[:, k, :], start=(n == 0), stop=(n == KB - 1))
        last.then_inc(s.logit_done, 1)
        pe.wait_ge(s.logit_sb, 1)
        for t in range(TT):
            last = pe.transpose(ps[:, 5, NE * t:NE * t + NE], lgt[:, P * t:P * t + P], ident[0:NE, 0:NE])
        last.then_inc(s.logit_t, 1)
        keep_warm(7, 26)
        pe.wait_ge(s.mask_ready, 1)
        g = dict(skip_group_check=True)
        mm(ps[:, 6, 0:NE], before[:], mask[:, 0, :], start=True, stop=True, **g)
        mm(ps[:, 6, NE:2 * NE], ones[:], mask[:, 0, :], start=True, stop=False, **g)
        mm(ps[:, 6, NE:2 * NE], before[:], mask[:, 1, :], start=False, stop=True, **g)
        mm(ps[:, 6, 2 * NE:3 * NE], ones[:], mask[:, 0, :], start=True, stop=False, **g)
        mm(ps[:, 6, 2 * NE:3 * NE], ones[:], mask[:, 1, :], start=False, stop=True, **g).then_inc(s.rank_done, 1)

        pe.sem_inc(s.acc_added, 4)

        def scatter():
            for j in range(4):
                t, c = divmod(j, 2)
                mm(ps[:, 2 + j, :], wpt[:, t, :], zsb[:, 512 * c:512 * c + 512], start=True,
                   stop=True).then_inc(s.scat_done, 1)

        def gather():
            for k in range(KB):
                for t in range(TT):
                    last = mm(ps[:, k // 4, P * (k % 4):P * (k % 4) + P], h1[:, t, P * k:P * k + P],
                              pick[:, t, :], start=(t == 0), stop=(t == 1))
            last.then_inc(s.gath_done, 1)

        keep_warm(7, 6)
        pe.wait_ge(s.pick_ready, TT)
        pe.wait_ge(s.h1_ready, 1)
        gather()
        pe.wait_ge(s.units_ready, 1)
        def unit(u, e, odd):

            def product(j, lhs, bank0, used):
                for q in range(4):
                    w = raw[:, ESLOT[j], 2 * q:2 * q + 2, :]
                    if j == 0 and odd:
                        w = gate_x[:, 2 * q:2 * q + 2, :]
                        pe.wait_ge(gate_x_in[q], e * 8 + 8)
                    elif j == 1 and q < 2 and odd:
                        w = up_x[q]
                        pe.wait_ge(up_x_in[q], e * 8 + 8)
                    elif j == 0 or j == 1 and q < 2:
                        pe.wait_ge(raw_in[ESLOT[j]][q], e * 8 + 16 * (LAP[j] + 1))
                    else:
                        pe.wait_ge(raw_in[ESLOT[j]][q], e * 16 + 16 * (LAP[j] + 1))
                    for c in range(2):
                        for k in (2 * q, 2 * q + 1):
                            r0 = SLOTS * (k % 2)
                            last = mm(ps[r0:r0 + SLOTS, bank0 + c, :], lhs[:, k, :],
                                      w[:, k % 2, 512 * c:512 * c + 512], start=(q == 0), stop=(q == 3))
                    last.then_inc(used, 1)

            pe.wait_ge(s.xg_ready, u + 1)
            pe.wait_ge(s.wpt_ready, u + 1)
            product(0, xg, 0, s.gate_used)
            pe.wait_ge(s.acc_added, u * 4 + 2)
            product(1, xg, 2, s.up_used)
            pe.wait_ge(s.gsb_ready, u * 2 + 2)
            pe.wait_ge(s.acc_added, u * 4 + 4)
            for k in range(KB):
                last = pe.transpose(ps[:, 4 + k // 4, P * (k % 4):P * (k % 4) + P], gsb[:, P * k:P * k + P], ident[:])
            last.then_inc(s.tg_done, 1)
            pe.wait_ge(s.usb_ready, u * 2 + 2)
            pe.wait_ge(s.z_ready, u * 2 + 2)
            for k in range(KB):
                last = pe.transpose(ps[:, 6 + k // 4, P * (k % 4):P * (k % 4) + P], usb[:, P * k:P * k + P], ident[:])
            last.then_inc(s.tu_done, 1)
            pe.wait_ge(s.gate_ready, u + 1)
            scatter()
            pe.wait_ge(s.wpick_ready, u * 2 + 2)
            for t in range(TT):
                last = pe.transpose(ps[:, 0, P * t:P * t + P], wpick[:, t, :], ident[:])
            last.then_inc(s.wpt_t, 1)
            pe.wait_ge(s.hid_ready, u + 1)
            product(2, hid, 6, s.down_used)
            pe.wait_ge(s.pick_ready, u * 2 + 4)
            pe.wait_ge(s.wpt_ready, u + 2)
            gather()

        with pe.Fori(0, NE // 2) as i:
            for odd in range(2):
                e = pe.snap(i * 2 + odd)
                blocks_of_e = pe.value_load(blocks[0:1, 0, bass.ds(e, 1)], min_val=1, max_val=MAXBLK)
                first = pe.value_load(blocks[0:1, 1, bass.ds(e, 1)], min_val=0, max_val=UNITS)
                with pe.Fori(0, blocks_of_e) as b:
                    unit(pe.snap(first + b), e, odd)
        count = pe.value_load(total[:], min_val=NE, max_val=UNITS - 2)
        pe.wait_ge(s.acc_added, count * 4 + 4)
        pe.wait_ge(s.wpt_ready, count + 1)
        pe.wait_ge(s.z_ready, count * 2 + 2)
        scatter()




_INS = ['x', 'meta_tokens', 'ln_in_g', 'ln_in_b', 'w_in', 'conv_w', 'conv_b', 'wq_m', 'wk_m', 'wv_m', 'b_i', 'b_f',
        'm_norm_g', 'lam_q1', 'lam_k1', 'lam_q2', 'lam_k2', 'a_norm_g', 'w_branch_m', 'w_branch_a', 'w_out',
        'ln1_g', 'ln1_b', 'ln2_g', 'ln2_b', 'w_router', 'router_bias', 'w_gate_e', 'w_up_e', 'w_down_e']
_OUTS = [((1, T, D), 'float32')]


def kernel(**inputs):
    import numpy as _np
    import concourse.bacc as _bacc
    from concourse.bass_utils import run_bass_kernel_spmd as _run

    nc = _bacc.Bacc("TRN2", target_bir_lowering=False, num_devices=1)
    arrays, args = {}, []
    for name in _INS:
        a = _np.ascontiguousarray(inputs[name])
        arrays[f"in_{name}_dram"] = a
        args.append(nc.dram_tensor(f"in_{name}_dram", a.shape, mybir.dt.from_np(a.dtype), kind="ExternalInput").ap())
    for i, (shape, dtype) in enumerate(_OUTS):
        dt = mybir.dt.from_np(_np.dtype(dtype))
        args.append(nc.dram_tensor(f"out_{i}_dram", shape, dt, kind="ExternalOutput").ap())
    with ExitStack() as ctx:
        build(ctx, nc, *args)
    r = _run(nc, [arrays], core_ids=[0])
    return r.results[0]["out_0_dram"]
```
